# Optimizing a Trainium2 kernel written in Bass

```python
import math
import jax, jax.numpy as jnp
from jax import lax
import numpy as np

D_MODEL = 1024
BATCH = 1
SEQ = 256
DEPTH = 2

N_A_LAYERS = DEPTH // 2
N_B_LAYERS = DEPTH - N_A_LAYERS
CONV_WIDTH = 3
FFN_HIDDEN = -(-8 * D_MODEL // (3 * 256)) * 256
N_HEADS = 16
N_KV_GROUPS = 4
HEADS_PER_GROUP = N_HEADS // N_KV_GROUPS
HEAD_DIM = 64
L_CMP = 32
D_CMP = 16
L_SLC = 64
N_SEL = 16
WINDOW = 512
CMP_HIDDEN = 256
Q_BLOCK = 64
N_KV_SETS = 6
RMS_EPS = 1e-5
NEG_INF = -1e30
FORCE_BONUS = 1e4


def rms_norm(x, g):
    xf = x.astype(jnp.float32)
    y = xf * lax.rsqrt(jnp.mean(xf * xf, axis=-1, keepdims=True) + RMS_EPS)
    return (y * g.astype(jnp.float32)).astype(x.dtype)

def short_conv_mixer(h, w_in, conv_w, w_out):
    b_gate, c_gate, v = jnp.split(h @ w_in, 3, axis=-1)
    u = lax.conv_general_dilated(
        c_gate * v, conv_w[:, None, :], window_strides=(1,),
        padding=((CONV_WIDTH - 1, 0),), dimension_numbers=("NWC", "WIO", "NWC"),
        feature_group_count=D_MODEL)
    return (b_gate * u) @ w_out

def swiglu(h, w_gu, w_down):
    g, u = jnp.split(h @ w_gu, 2, axis=-1)
    return (jax.nn.silu(g) * u) @ w_down

def compress(kv_raw, pe, w1, w2):
    bsz, seq = kv_raw.shape[0], kv_raw.shape[1]
    n_cmp = (seq - L_CMP) // D_CMP + 1
    idx = jnp.arange(n_cmp)[:, None] * D_CMP + jnp.arange(L_CMP)[None, :]
    blocks = kv_raw[:, idx] + pe[None, None, :, None, :]
    blocks = blocks.transpose(0, 1, 3, 2, 4).reshape(bsz, n_cmp, N_KV_GROUPS, L_CMP * HEAD_DIM)
    return jax.nn.silu(blocks @ w1) @ w2

def shared_kv(h, kv_norm, w_kv, pe_k, w1_k, w2_k, pe_v, w1_v, w2_v):
    bsz, seq, _ = h.shape
    kv = (rms_norm(h, kv_norm) @ w_kv).reshape(bsz, seq, N_KV_SETS, N_KV_GROUPS, HEAD_DIM)
    k_cmp = compress(kv[:, :, 0], pe_k, w1_k, w2_k)
    v_cmp = compress(kv[:, :, 1], pe_v, w1_v, w2_v)
    return (k_cmp, v_cmp, kv[:, :, 2], kv[:, :, 3], kv[:, :, 4], kv[:, :, 5])

def nsa_mixer(h, w_qg, w_o, k_cmp, v_cmp, k_slc, v_slc, k_win, v_win):
    bsz, seq, _ = h.shape
    G, HPG, dh = N_KV_GROUPS, HEADS_PER_GROUP, HEAD_DIM
    qg = h @ w_qg
    q = (qg[..., :N_HEADS * dh] * (dh ** -0.5)).reshape(bsz, seq, G, HPG, dh)
    gates = jax.nn.sigmoid(qg[..., N_HEADS * dh:].astype(jnp.float32)).reshape(bsz, seq, G, HPG, 3)

    slopes = jnp.exp2(-8.0 * jnp.arange(1, N_HEADS + 1, dtype=jnp.float32) / N_HEADS).reshape(G, HPG)

    n_cmp = k_cmp.shape[1]
    cmp_start = jnp.arange(n_cmp) * D_CMP
    cmp_end = cmp_start + L_CMP - 1
    cmp_center = cmp_end.astype(jnp.float32) - (L_CMP - 1) / 2.0
    n_slc = seq // L_SLC
    n_sel = min(N_SEL, n_slc)
    slc_start = jnp.arange(n_slc) * L_SLC
    overlap = ((cmp_start[:, None] < slc_start[None, :] + L_SLC)
               & (cmp_start[:, None] + L_CMP > slc_start[None, :])).astype(jnp.float32)

    k_blk = k_slc.reshape(bsz, n_slc, L_SLC, G, dh).transpose(0, 3, 1, 2, 4)
    v_blk = v_slc.reshape(bsz, n_slc, L_SLC, G, dh).transpose(0, 3, 1, 2, 4)
    pad = ((0, 0), (WINDOW, 0), (0, 0), (0, 0))
    k_win_pad = jnp.pad(k_win, pad)
    v_win_pad = jnp.pad(v_win, pad)
    b_ix = jnp.arange(bsz)[:, None, None, None]
    g_ix = jnp.arange(G)[None, :, None, None]
    j_blk = jnp.arange(n_slc)

    def one_block(qb):
        q0 = qb * Q_BLOCK
        t = q0 + jnp.arange(Q_BLOCK)
        tf = t.astype(jnp.float32)
        qblk = lax.dynamic_slice_in_dim(q, q0, Q_BLOCK, axis=1)
        gblk = lax.dynamic_slice_in_dim(gates, q0, Q_BLOCK, axis=1)

        s = jnp.einsum("bqghd,bngd->bghqn", qblk, k_cmp).astype(jnp.float32)
        vis = cmp_end[None, :] <= t[:, None]
        s = s - slopes[:, :, None, None] * (tf[:, None] - cmp_center[None, :])
        p_cmp = jax.nn.softmax(jnp.where(vis, s, NEG_INF), axis=-1) * vis
        o_cmp = jnp.einsum("bghqn,bngd->bqghd", p_cmp.astype(v_cmp.dtype), v_cmp)

        imp = jnp.einsum("bghqn,nj->bgqj", p_cmp, overlap)
        cur = t // L_SLC
        valid = j_blk[None, :] <= cur[:, None]
        forced = ((j_blk[None, :] == 0) | (j_blk[None, :] == cur[:, None])
                  | (j_blk[None, :] == cur[:, None] - 1))
        imp = jnp.where(valid, imp + FORCE_BONUS * forced, NEG_INF)
        _, sel = lax.top_k(imp, n_sel)
        k_sel = k_blk[b_ix, g_ix, sel]
        v_sel = v_blk[b_ix, g_ix, sel]
        s = jnp.einsum("bqghd,bgqnld->bghqnl", qblk, k_sel).astype(jnp.float32)
        dist = t[None, None, :, None, None] - (sel[..., None] * L_SLC + jnp.arange(L_SLC))
        dist = dist[:, :, None]
        s = s - slopes[:, :, None, None, None] * dist.astype(jnp.float32)
        s = jnp.where(dist >= 0, s, NEG_INF)
        p = jax.nn.softmax(s.reshape(s.shape[:4] + (n_sel * L_SLC,)), axis=-1).reshape(s.shape)
        o_slc = jnp.einsum("bghqnl,bgqnld->bqghd", p.astype(v_sel.dtype), v_sel)

        kw = lax.dynamic_slice_in_dim(k_win_pad, q0, WINDOW + Q_BLOCK, axis=1)
        vw = lax.dynamic_slice_in_dim(v_win_pad, q0, WINDOW + Q_BLOCK, axis=1)
        spos = q0 - WINDOW + jnp.arange(WINDOW + Q_BLOCK)
        d = t[:, None] - spos[None, :]
        m = (d >= 0) & (d < WINDOW) & (spos >= 0)[None, :]
        s = jnp.einsum("bqghd,bkgd->bghqk", qblk, kw).astype(jnp.float32)
        s = s - slopes[:, :, None, None] * d.astype(jnp.float32)
        p = jax.nn.softmax(jnp.where(m, s, NEG_INF), axis=-1)
        o_win = jnp.einsum("bghqk,bkgd->bqghd", p.astype(vw.dtype), vw)

        o = (gblk[..., 0:1] * o_cmp + gblk[..., 1:2] * o_slc + gblk[..., 2:3] * o_win)
        return o.reshape(bsz, Q_BLOCK, N_HEADS * dh).astype(h.dtype)

    out = lax.map(one_block, jnp.arange(seq // Q_BLOCK))
    out = out.transpose(1, 0, 2, 3).reshape(bsz, seq, N_HEADS * dh)
    return out @ w_o

def first_inputs(seed: int = 0) -> dict:
    key = jax.random.key(seed)
    ks = jax.random.split(key, 24)

    def w(k, shape, fan_in):
        return jax.random.normal(k, shape, jnp.float32) * (fan_in ** -0.5)

    def gain(k, shape):
        return 1.0 + 0.02 * jax.random.normal(k, shape, jnp.float32)

    D, F = D_MODEL, FFN_HIDDEN
    kv_w = N_KV_GROUPS * HEAD_DIM
    qg_w = N_HEADS * HEAD_DIM + 3 * N_HEADS
    return {
        "x": jax.random.normal(ks[0], (BATCH, SEQ, D), jnp.float32),
        "a_norm": gain(ks[1], (N_A_LAYERS, D)),
        "a_w_in": w(ks[2], (N_A_LAYERS, D, 3 * D), D),
        "a_conv": w(ks[3], (N_A_LAYERS, CONV_WIDTH, D), CONV_WIDTH),
        "a_w_out": w(ks[4], (N_A_LAYERS, D, D), D),
        "kv_norm": gain(ks[5], (D,)),
        "w_kv": w(ks[6], (D, N_KV_SETS * kv_w), D),
        "cmp_pe_k": 0.02 * jax.random.normal(ks[7], (L_CMP, HEAD_DIM), jnp.float32),
        "cmp_w1_k": w(ks[8], (L_CMP * HEAD_DIM, CMP_HIDDEN), L_CMP * HEAD_DIM),
        "cmp_w2_k": w(ks[9], (CMP_HIDDEN, HEAD_DIM), CMP_HIDDEN),
        "cmp_pe_v": 0.02 * jax.random.normal(ks[10], (L_CMP, HEAD_DIM), jnp.float32),
        "cmp_w1_v": w(ks[11], (L_CMP * HEAD_DIM, CMP_HIDDEN), L_CMP * HEAD_DIM),
        "cmp_w2_v": w(ks[12], (CMP_HIDDEN, HEAD_DIM), CMP_HIDDEN),
        "b_norm": gain(ks[13], (N_B_LAYERS, D)),
        "b_w_qg": w(ks[14], (N_B_LAYERS, D, qg_w), D),
        "b_w_o": w(ks[15], (N_B_LAYERS, N_HEADS * HEAD_DIM, D), N_HEADS * HEAD_DIM),
        "f_norm": gain(ks[16], (DEPTH, D)),
        "f_w_gu": w(ks[17], (DEPTH, D, 2 * F), D),
        "f_w_down": w(ks[18], (DEPTH, F, D), F),
        "final_norm": gain(ks[19], (D,)),
    }

def first_block(x, a_norm, a_w_in, a_conv, a_w_out, kv_norm, w_kv, cmp_pe_k, cmp_w1_k, cmp_w2_k,
              cmp_pe_v, cmp_w1_v, cmp_w2_v, b_norm, b_w_qg, b_w_o, f_norm, f_w_gu, f_w_down,
              final_norm):
    h = x
    shared = None
    for layer in range(DEPTH):
        if layer < N_A_LAYERS:
            i = layer
            h = h + short_conv_mixer(rms_norm(h, a_norm[i]), a_w_in[i], a_conv[i], a_w_out[i])
        else:
            i = layer - N_A_LAYERS
            if shared is None:
                shared = shared_kv(h, kv_norm, w_kv, cmp_pe_k, cmp_w1_k, cmp_w2_k,
                                   cmp_pe_v, cmp_w1_v, cmp_w2_v)
            k_cmp, v_cmp, k_slc, v_slc, k_win, v_win = shared
            h = h + nsa_mixer(rms_norm(h, b_norm[i]), b_w_qg[i], b_w_o[i],
                              k_cmp, v_cmp, k_slc, v_slc, k_win, v_win)
        h = h + swiglu(rms_norm(h, f_norm[layer]), f_w_gu[layer], f_w_down[layer])
    return rms_norm(h, final_norm)


DEPTH_2 = 1

ATTN_WIDTH = D_MODEL // 2
ATTN_HEAD_DIM = 64
N_ATTN_HEADS = ATTN_WIDTH // ATTN_HEAD_DIM
MLSTM_WIDTH = D_MODEL - ATTN_WIDTH
N_MLSTM_HEADS = 4
MLSTM_HEAD_DIM = MLSTM_WIDTH // N_MLSTM_HEADS
MLSTM_CHUNK = 64
CONV_WIDTH_2 = 4
DILATED_PATTERNS = ((128, 1), (512, 4), (2048, 16))
ATTN_BLOCK = 128
ATTN_SCALE = ATTN_HEAD_DIM ** -0.5
D_FF = ((8 * D_MODEL // 3 + 255) // 256) * 256
N_MOD = 6
RMS_EPS_2 = 1e-6
IN_SPLITS = (ATTN_WIDTH, ATTN_WIDTH, ATTN_WIDTH,
             MLSTM_WIDTH, MLSTM_WIDTH, MLSTM_WIDTH,
             MLSTM_WIDTH,
             N_MLSTM_HEADS, N_MLSTM_HEADS)
IN_COLS = sum(IN_SPLITS)


def rms_norm_2(x, g):
    xf = x.astype(jnp.float32)
    y = xf * lax.rsqrt(jnp.mean(xf * xf, axis=-1, keepdims=True) + RMS_EPS_2)
    return (y * g.astype(jnp.float32)).astype(x.dtype)

def modulate(h, shift, scale):
    return h * (1 + scale[:, None, :]) + shift[:, None, :]

def causal_short_conv(x, w, b):
    S = x.shape[1]
    xp = jnp.pad(x, ((0, 0), (CONV_WIDTH_2 - 1, 0), (0, 0)))
    y = b
    for j in range(CONV_WIDTH_2):
        y = y + xp[:, j:j + S] * w[j]
    return y

def dilated_branch(q, k, v, window, dilation):
    B, S, H, Dh = q.shape
    n_back = window // dilation
    assert n_back <= ATTN_BLOCK and S % dilation == 0
    L = S // dilation
    nb = -(-L // ATTN_BLOCK)
    Lp = nb * ATTN_BLOCK

    def to_sub(t):
        t = t.reshape(B, L, dilation, H, Dh).transpose(0, 2, 1, 3, 4)
        t = jnp.pad(t, ((0, 0), (0, 0), (0, Lp - L), (0, 0), (0, 0)))
        return t.reshape(B, dilation, nb, ATTN_BLOCK, H, Dh)

    def with_prev(t):
        prev = jnp.pad(t, ((0, 0), (0, 0), (1, 0), (0, 0), (0, 0), (0, 0)))[:, :, :-1]
        return jnp.concatenate([prev, t], axis=3)

    qb = to_sub(q)
    kb = with_prev(to_sub(k))
    vb = with_prev(to_sub(v))
    s = jnp.einsum('brnqhd,brnkhd->brnhqk', qb, kb).astype(jnp.float32)
    qi = jnp.arange(ATTN_BLOCK)[:, None] + ATTN_BLOCK
    kj = jnp.arange(2 * ATTN_BLOCK)[None, :]
    rel = qi - kj
    band = (rel >= 0) & (rel <= n_back)
    valid = band[None] & ((jnp.arange(nb)[:, None, None] > 0) | (kj[None] >= ATTN_BLOCK))
    s = jnp.where(valid[None, None, :, None], s, -jnp.inf)
    lse = jax.nn.logsumexp(s, axis=-1)
    p = jnp.exp(s - lse[..., None])
    o = jnp.einsum('brnhqk,brnkhd->brnqhd', p.astype(v.dtype), vb)
    o = o.reshape(B, dilation, Lp, H, Dh)[:, :, :L]
    o = o.transpose(0, 2, 1, 3, 4).reshape(B, S, H, Dh)
    lse = lse.transpose(0, 1, 2, 4, 3).reshape(B, dilation, Lp, H)[:, :, :L]
    lse = lse.transpose(0, 2, 1, 3).reshape(B, S, H)
    return o, lse

def dilated_attention(q, k, v):
    outs, lses = [], []
    for window, dilation in DILATED_PATTERNS:
        o, lse = dilated_branch(q, k, v, window, dilation)
        outs.append(o)
        lses.append(lse)
    w = jax.nn.softmax(jnp.stack(lses, axis=0), axis=0)
    return jnp.einsum('pbsh,pbshd->bshd', w.astype(v.dtype), jnp.stack(outs, axis=0))

def mlstm_chunkwise(q, k, v, log_i, log_f):
    B, NH, S, D = q.shape
    L = MLSTM_CHUNK
    NC = S // L
    k = k * (D ** -0.5)

    def to_chunks(t):
        return jnp.moveaxis(t.reshape(B, NH, NC, L, *t.shape[3:]), 2, 0)

    xs = (to_chunks(q), to_chunks(k), to_chunks(v), to_chunks(log_i), to_chunks(log_f))
    causal = jnp.tril(jnp.ones((L, L), dtype=bool))

    def step(carry, inp):
        C, n, m = carry
        qc, kc, vc, ic, fc = inp
        b = jnp.cumsum(fc, axis=-1)
        log_d = b[..., :, None] - b[..., None, :] + ic[..., None, :]
        log_d = jnp.where(causal, log_d, -jnp.inf)
        m_inter = b + m[..., None]
        m_t = jnp.maximum(m_inter, jnp.max(log_d, axis=-1))
        d_mat = jnp.exp(log_d - m_t[..., None])
        inter = jnp.exp(m_inter - m_t)
        s_qk = jnp.einsum('bhtd,bhsd->bhts', qc, kc) * d_mat
        num = inter[..., None] * jnp.einsum('bhtd,bhde->bhte', qc, C) + jnp.einsum('bhts,bhse->bhte', s_qk, vc)
        nq = inter * jnp.einsum('bhtd,bhd->bht', qc, n) + jnp.sum(s_qk, axis=-1)
        h = num / jnp.maximum(jnp.abs(nq), jnp.exp(-m_t))[..., None]
        b_last = b[..., -1]
        w_log = b_last[..., None] - b + ic
        m_new = jnp.maximum(b_last + m, jnp.max(w_log, axis=-1))
        w = jnp.exp(w_log - m_new[..., None])
        decay = jnp.exp(b_last + m - m_new)
        C_new = decay[..., None, None] * C + jnp.einsum('bhs,bhsd,bhse->bhde', w, kc, vc)
        n_new = decay[..., None] * n + jnp.einsum('bhs,bhsd->bhd', w, kc)
        return (C_new, n_new, m_new), h

    init = (jnp.zeros((B, NH, D, D), jnp.float32),
            jnp.zeros((B, NH, D), jnp.float32),
            jnp.zeros((B, NH), jnp.float32))
    _, h = lax.scan(step, init, xs)
    return jnp.moveaxis(h, 0, 2).reshape(B, NH, S, D)

def token_mixer(h, w_in, w_conv, b_conv, b_igate, b_fgate, q_norm_g, k_norm_g, mlstm_norm_g, w_out):
    B, S, _ = h.shape
    xin = h @ w_in
    cuts = list(np.cumsum(IN_SPLITS)[:-1])
    qa, ka, va, qm, km, vm, og, ig, fg = jnp.split(xin, cuts, axis=-1)
    qa = rms_norm_2(qa.reshape(B, S, N_ATTN_HEADS, ATTN_HEAD_DIM), q_norm_g) * ATTN_SCALE
    ka = rms_norm_2(ka.reshape(B, S, N_ATTN_HEADS, ATTN_HEAD_DIM), k_norm_g)
    va = va.reshape(B, S, N_ATTN_HEADS, ATTN_HEAD_DIM)
    attn = dilated_attention(qa, ka, va).reshape(B, S, ATTN_WIDTH)
    qkm = jax.nn.silu(causal_short_conv(jnp.concatenate([qm, km], axis=-1), w_conv, b_conv))
    qm, km = jnp.split(qkm, 2, axis=-1)

    def heads(t):
        return t.reshape(B, S, N_MLSTM_HEADS, MLSTM_HEAD_DIM).transpose(0, 2, 1, 3).astype(jnp.float32)

    log_i = (ig + b_igate).astype(jnp.float32).transpose(0, 2, 1)
    log_f = jax.nn.log_sigmoid((fg + b_fgate).astype(jnp.float32)).transpose(0, 2, 1)
    hm = mlstm_chunkwise(heads(qm), heads(km), heads(vm), log_i, log_f)
    hm = hm.transpose(0, 2, 1, 3).astype(h.dtype)
    hm = rms_norm_2(hm, mlstm_norm_g.reshape(N_MLSTM_HEADS, MLSTM_HEAD_DIM)).reshape(B, S, MLSTM_WIDTH)
    hm = jax.nn.sigmoid(og) * hm
    return jnp.concatenate([attn, hm], axis=-1) @ w_out

def swiglu_2(h, w_gate, w_up, w_down):
    return (jax.nn.silu(h @ w_gate) * (h @ w_up)) @ w_down

def second_inputs(seed: int = 0) -> dict:
    key = jax.random.key(seed)
    ks = jax.random.split(key, 20)
    f32 = jnp.float32
    D = D_MODEL

    def nrm(k, shape, scale):
        return jax.random.normal(k, shape, f32) * scale

    b_ada = nrm(ks[15], (DEPTH_2, N_MOD * D), 0.02)
    gate_cols = jnp.zeros((N_MOD, D), f32).at[2].set(1.0).at[5].set(1.0).reshape(-1)
    b_ada = b_ada + gate_cols
    f_bias = jnp.linspace(3.0, 6.0, N_MLSTM_HEADS, dtype=f32)[None, :]
    return {
        "x": nrm(ks[0], (BATCH, SEQ, D), 1.0),
        "c": nrm(ks[1], (BATCH, D), 1.0),
        "g_mix": 1.0 + nrm(ks[2], (DEPTH_2, D), 0.02),
        "w_in": nrm(ks[3], (DEPTH_2, D, IN_COLS), D ** -0.5),
        "w_conv": nrm(ks[4], (DEPTH_2, CONV_WIDTH_2, 2 * MLSTM_WIDTH), CONV_WIDTH_2 ** -0.5),
        "b_conv": nrm(ks[5], (DEPTH_2, 2 * MLSTM_WIDTH), 0.02),
        "b_igate": nrm(ks[6], (DEPTH_2, N_MLSTM_HEADS), 0.1),
        "b_fgate": f_bias + nrm(ks[7], (DEPTH_2, N_MLSTM_HEADS), 0.1),
        "q_norm_g": 1.0 + nrm(ks[8], (DEPTH_2, ATTN_HEAD_DIM), 0.02),
        "k_norm_g": 1.0 + nrm(ks[9], (DEPTH_2, ATTN_HEAD_DIM), 0.02),
        "mlstm_norm_g": 1.0 + nrm(ks[10], (DEPTH_2, MLSTM_WIDTH), 0.02),
        "w_out": nrm(ks[11], (DEPTH_2, D, D), D ** -0.5),
        "g_ffn": 1.0 + nrm(ks[12], (DEPTH_2, D), 0.02),
        "w_gate": nrm(ks[13], (DEPTH_2, D, D_FF), D ** -0.5),
        "w_up": nrm(ks[14], (DEPTH_2, D, D_FF), D ** -0.5),
        "w_down": nrm(ks[16], (DEPTH_2, D_FF, D), D_FF ** -0.5),
        "w_ada": nrm(ks[17], (DEPTH_2, D, N_MOD * D), 0.1 * D ** -0.5),
        "b_ada": b_ada,
    }

def second_block(x, c, g_mix, w_in, w_conv, b_conv, b_igate, b_fgate, q_norm_g, k_norm_g,
              mlstm_norm_g, w_out, g_ffn, w_gate, w_up, w_down, w_ada, b_ada):
    for l in range(DEPTH_2):
        mod = jax.nn.silu(c) @ w_ada[l] + b_ada[l]
        sh_m, sc_m, gt_m, sh_f, sc_f, gt_f = jnp.split(mod, N_MOD, axis=-1)
        h = modulate(rms_norm_2(x, g_mix[l]), sh_m, sc_m)
        y = token_mixer(h, w_in[l], w_conv[l], b_conv[l], b_igate[l], b_fgate[l],
                        q_norm_g[l], k_norm_g[l], mlstm_norm_g[l], w_out[l])
        x = x + gt_m[:, None, :] * y
        h = modulate(rms_norm_2(x, g_ffn[l]), sh_f, sc_f)
        x = x + gt_f[:, None, :] * swiglu_2(h, w_gate[l], w_up[l], w_down[l])
    return x


def setup_inputs(seed=0):
    out = dict(first_inputs(seed))
    for name, value in second_inputs(seed + 1).items():
        if name != "x":
            out[name + "_2"] = value
    return out


def reference(
    x, a_norm, a_w_in, a_conv, a_w_out, kv_norm, w_kv, cmp_pe_k, cmp_w1_k, cmp_w2_k, cmp_pe_v,
    cmp_w1_v, cmp_w2_v, b_norm, b_w_qg, b_w_o, f_norm, f_w_gu, f_w_down, final_norm, c_2,
    g_mix_2, w_in_2, w_conv_2, b_conv_2, b_igate_2, b_fgate_2, q_norm_g_2, k_norm_g_2,
    mlstm_norm_g_2, w_out_2, g_ffn_2, w_gate_2, w_up_2, w_down_2, w_ada_2, b_ada_2,
):
    x = first_block(
        x, a_norm, a_w_in, a_conv, a_w_out, kv_norm, w_kv, cmp_pe_k, cmp_w1_k, cmp_w2_k,
        cmp_pe_v, cmp_w1_v, cmp_w2_v, b_norm, b_w_qg, b_w_o, f_norm, f_w_gu, f_w_down,
        final_norm,
    )
    return second_block(
        x, c_2, g_mix_2, w_in_2, w_conv_2, b_conv_2, b_igate_2, b_fgate_2, q_norm_g_2,
        k_norm_g_2, mlstm_norm_g_2, w_out_2, g_ffn_2, w_gate_2, w_up_2, w_down_2, w_ada_2,
        b_ada_2,
    )


_drawn_inputs = setup_inputs


def setup_inputs(seed=0):
    import zlib

    import numpy as np

    out = dict(_drawn_inputs(seed))
    spreads = {}
    factors = {'kv_norm': 7.14,
     'cmp_pe_k': 8.0,
     'cmp_pe_v': 8.0,
     'b_norm': 8.0,
     'f_norm': 2.959,
     'g_mix_2': 4.337,
     'b_conv_2': 64.0,
     'b_igate_2': 200.0,
     'q_norm_g_2': 8.0,
     'k_norm_g_2': 8.0,
     'mlstm_norm_g_2': 19.65,
     'g_ffn_2': 4.078}
    for name, (base, spread) in spreads.items():
        noise = np.random.default_rng([zlib.crc32(name.encode()), seed]).standard_normal(out[name].shape)
        drawn = base * np.exp(spread * noise) if base else spread * noise
        out[name] = __import__('jax').numpy.asarray(drawn.astype(out[name].dtype))
    for name, factor in factors.items():
        out[name] = (out[name] * factor).astype(out[name].dtype)
    return out
```

```python
from contextlib import ExitStack

import concourse.bass as bass
from concourse import mybir

F32 = mybir.dt.float32
F32R = mybir.dt.float32r
ALU = mybir.AluOpType
ACT = mybir.ActivationFunctionType
AX_X = mybir.AxisListType.X

P = 128
T = 256
TT = T // P
D = 1024
KT = D // P
FFN = 2816
FT = FFN // P
NH, NG = 16, 4
HD = 64
NH2 = 8
NM = 4
NEG = -1e30
SLOPES = [2.0 ** (-8.0 * (h + 1) / NH) for h in range(NH)]

ROWS, NROWS = {}, 0
for _name, _n in (("a_norm", 8), ("kv_norm", 8), ("b_norm", 8), ("f_norm", 16), ("final_norm", 8),
                  ("g_mix_2", 8), ("g_ffn_2", 8), ("c_2", 8), ("a_conv", 24), ("w_conv_2", 32),
                  ("b_conv_2", 8), ("b_ada_2", 48), ("mlstm_norm_g_2", 4), ("cmp_pe_k", 16),
                  ("cmp_pe_v", 16)):
    ROWS[_name] = NROWS
    NROWS += _n
ROWS["q_norm_g_2"], ROWS["k_norm_g_2"] = NROWS, NROWS + 1
NROWS += 2
N_PARAM_DMAS = 15 + 4

CV, BG, AO = 0, 8, 12
F0 = 16
KV = F0 + FT
QG = KV + 6
WO = QG + 4
F1 = WO + 4
MX = F1 + FT
MO = MX + 14
F2 = MO + 4
GTOTAL = F2 + FT
FFNS = (F0, F1, F2)
MX_QA, MX_KA, MX_VA, MX_QM, MX_KM, MX_VM, MX_OG = (MX + 2 * n for n in range(7))


def plan_chunks():
    chunks, chunk_of = [], {}

    def steps(first, n, pair):
        for g in range(first, first + n, 2):
            chunk_of[g] = chunk_of[g + 1] = len(chunks)
            chunks.append(("pair" if pair else "flat", g))

    steps(CV, 8, True)
    steps(BG, 4, False)
    steps(AO, 4, False)
    steps(F0, FT, True)
    steps(KV, 6, False)
    chunks.append(("cmp", 0))
    chunks.append(("cmp", 1))
    steps(QG, 4, False)
    steps(WO, 4, False)
    steps(F1, FT, True)
    steps(MX, 14, False)
    steps(MO, 4, False)
    steps(F2, FT, True)
    return chunks, chunk_of


CHUNKS, CHUNK_OF = plan_chunks()


def layer_kernel(nc, t, out, last_stage=7):
    ctx = ExitStack()

    def sb(name, shape, dt=F32, on=ctx):
        return on.enter_context(nc.sbuf_tensor(name, shape, dt))

    def sem(name):
        return ctx.enter_context(nc.semaphore(name))

    g_raw = sb("g_raw", [P, 2, KT, 512])
    g_hi = sb("g_hi", [P, 2, KT, 256], F32R)
    g_lo = sb("g_lo", [P, 2, KT, 256], F32R)
    xres = sb("xres", [P, KT, T])
    opa_hi = sb("opa_hi", [P, KT, T], F32R)
    opa_lo = sb("opa_lo", [P, KT, T], F32R)
    ybuf = sb("ybuf", [P, KT, T])
    silu_g = sb("silu_g", [P, 2, T])
    hid = sb("hid", [P, 2, T])
    hid_hi = sb("hid_hi", [P, 2, T], F32R)
    hid_lo = sb("hid_lo", [P, 2, T], F32R)
    rstd = sb("rstd", [P, T])
    ident = sb("ident", [P, P])
    ones = sb("ones", [P, P])
    ones64 = sb("ones64", [P, P])
    eps = sb("eps", [P, 2])
    par = sb("par", [P, NROWS])
    csil = sb("csil", [P, KT])
    mod = sb("mod", [P, 48])
    gmod = sb("gmod", [P, 16])
    zpad = sb("zpad", [P, 2, T + 4])
    qg_raw = sb("qg_raw", [P, KT, 48])
    qg_hi = sb("qg_hi", [P, KT, 48], F32R)
    qg_lo = sb("qg_lo", [P, KT, 48], F32R)
    if_raw = sb("if_raw", [P, KT, 8])
    if_hi = sb("if_hi", [P, KT, 8], F32R)
    if_lo = sb("if_lo", [P, KT, 8], F32R)
    if_bias = sb("if_bias", [P, 8])
    gates = sb("gates", [P, TT, 48])
    nmax = sb("nmax", [P, 3, 4])
    zsum = sb("zsum", [P, 3, 4])
    fac = sb("fac", [P, 3, 4])
    dist = sb("dist", [P, 384])
    cmp_bias = sb("cmp_bias", [P, 2, TT, 8, 16])
    any_vis = sb("any_vis", [P, TT])
    dil_count = sb("dil_count", [P, 384])
    dil_mask = sb("dil_mask", [P, 384])
    lstm_mask = sb("lstm_mask", [P, 384])
    sel4 = sb("sel4", [NM, NM, P])
    small = sb("small", [P, 64])
    cfac = sb("cfac", [P, 2, TT, 8])

    over = ExitStack()
    ada_acc = sb("ada_acc", [P, 6 * D], on=over)
    ada_raw = sb("ada_raw", [P, 2, D], on=over)
    over.close()
    over = ExitStack()
    qk_a = sb("qk_a", [P, KT, T], on=over)
    v_a = sb("v_a", [P, TT, 512], on=over)
    qk_m = sb("qk_m", [P, KT, T], on=over)
    v_m = sb("v_m", [P, TT, 512], on=over)
    og_s = sb("og_s", [P, NM, T], on=over)
    if_tok = sb("if_tok", [P, TT, 8], on=over)
    if_tmp = sb("if_tmp", [P, TT, 3, 4], on=over)
    a_col = sb("a_col", [P, TT, NM], on=over)
    comb = sb("comb", [16, 2, T], on=over)
    sb("pad_a", [P, 8192 - 7168 - 16 - 24 - 8 - 512], on=over)
    ctx.push(over)

    over_b = ExitStack()
    opb_hi = sb("opb_hi", [P, KT, T], F32R, on=over_b)
    opb_lo = sb("opb_lo", [P, KT, T], F32R, on=over_b)
    d_raw = sb("d_raw", [P, 2, 2, D], on=over_b)
    d_hi = sb("d_hi", [P, 2, D], F32R, on=over_b)
    d_lo = sb("d_lo", [P, 2, D], F32R, on=over_b)
    over_b.close()
    over_b = ExitStack()
    e_buf = sb("e_buf", [P, 3, 768], on=over_b)
    pt_buf = sb("pt_buf", [P, 2, 384], on=over_b)
    bias_h = sb("bias_h", [P, 2, 384], on=over_b)
    sb("pad_b", [P, 4096 - 3840], on=over_b)
    k_dup = sb("k_dup", [P, 2, NG, T], on=over_b)
    v_tok = sb("v_tok", [P, 2, TT, T], on=over_b)
    x_cmp = sb("x_cmp", [P, 2, NG, 288], on=over_b)
    b_cmp = sb("b_cmp", [P, 16, NG, 16], on=over_b)
    vc_blk = sb("vc_blk", [P, 8, HD], on=over_b)
    hid_cmp = sb("hid_cmp", [P, 2, 2, NG, 16], on=over_b)
    kc_dup = sb("kc_dup", [P, NG, 16], on=over_b)
    w2_k = sb("w2_k", [P, 2, 2, HD], on=over_b)
    w2_v = sb("w2_v", [P, 2, HD], on=over_b)
    over_b.close()
    over_b = ExitStack()
    e_dil = sb("e_dil", [P, 3, 384], on=over_b)
    pt_dil = sb("pt_dil", [P, 2, 384], on=over_b)
    qk_rt = sb("qk_rt", [P, 2, T], on=over_b)
    rows = sb("rows", [NM, 7, T], on=over_b)
    ones_row = sb("ones_row", [NM, T], on=over_b)
    decay = sb("decay", [P, 2, 384], on=over_b)
    s_lstm = sb("s_lstm", [P, 2, 384], on=over_b)
    l_abs = sb("l_abs", [P, 2, T], on=over_b)
    l_emt = sb("l_emt", [P, 2, T], on=over_b)
    l_num = sb("l_num", [P, 2, T], on=over_b)
    l_sq = sb("l_sq", [P, 2, T], on=over_b)
    mix = sb("mix", [P, KT, T], on=over_b)
    over_b.close()
    over_b = ExitStack()
    prow = sb("prow", [P, 2, P], on=over_b)
    over_b.close()
    sb("over_b_extent", [P, 12288])

    ps = ctx.enter_context(nc.psum_tensor("ps", [P, 8, 512], F32))

    x_loaded, par_loaded, side_loaded = sem("x_loaded"), sem("par_loaded"), sem("side_loaded")
    g_loaded = [sem("g_loaded0"), sem("g_loaded1")]
    d_loaded = [sem("d_loaded0"), sem("d_loaded1")]
    ada_loaded = [sem("ada_loaded0"), sem("ada_loaded1")]
    w2_loaded = sem("w2_loaded")
    stored = sem("stored")
    consts = sem("consts")
    g_hi_made, g_lo_made = sem("g_hi_made"), sem("g_lo_made")
    d_hi_made, d_lo_made = sem("d_hi_made"), sem("d_lo_made")
    side_hi, side_lo = sem("side_hi"), sem("side_lo")
    g_done, g_evac = sem("g_done"), sem("g_evac")
    d_done = sem("d_done")
    opa_hi_made, opa_made = sem("opa_hi_made"), sem("opa_made")
    opb_hi_made, opb_made = sem("opb_hi_made"), sem("opb_made")
    x_turned, xres_made = sem("x_turned"), sem("xres_made")
    par_turned, par_made = sem("par_turned"), sem("par_made")
    csil_made = sem("csil_made")
    ada_scaled, ada_added, ada_summed, mod_made = sem("ada_scaled"), sem("ada_added"), sem("ada_summed"), sem("mod_made")
    res_added = sem("res_added")
    sq_made, ss_done, rms_made = sem("sq_made"), sem("ss_done"), sem("rms_made")
    y_made = sem("y_made")
    c_copied = sem("c_copied")
    silu_made, hid_made, hid_hi_made, hid_lo_made = (sem("silu_made"), sem("hid_made"),
                                                     sem("hid_hi_made"), sem("hid_lo_made"))
    kv_copied = sem("kv_copied")
    b_cmp_made, cmp_hid_done, cmp_hid_silu = sem("b_cmp_made"), sem("cmp_hid_done"), sem("cmp_hid_silu")
    kc_done, kc_made = sem("kc_done"), sem("kc_made")
    gate_done, gate_exp, gates_made = sem("gate_done"), sem("gate_exp"), sem("gates_made")
    cs_done, cs_shift, cs_exp, cs_made = sem("cs_done"), sem("cs_shift"), sem("cs_exp"), sem("cs_made")
    pct_done, pct_made = sem("pct_done"), sem("pct_made")
    bias_made = sem("bias_made")
    scored, shifted, exp_made, fac_made, scaled = (sem("scored"), sem("shifted"), sem("exp_made"),
                                                   sem("fac_made"), sem("scaled"))
    pt_done, pt_slc, pt_win, pv_done = sem("pt_done"), sem("pt_slc"), sem("pt_win"), sem("pv_done")
    comb_done = sem("comb_done")
    z_copied, conv_made = sem("z_copied"), sem("conv_made")
    qk_sq, qk_ss, qk_root, qk_made = sem("qk_sq"), sem("qk_ss"), sem("qk_root"), sem("qk_made")
    og_exp = sem("og_exp")
    if_done, if_in, if_abs, if_tok_made = sem("if_done"), sem("if_in"), sem("if_abs"), sem("if_tok_made")
    rows_turned, rows_made, a_turned, a_made = (sem("rows_turned"), sem("rows_made"),
                                                sem("a_turned"), sem("a_made"))
    m_cast, arg_made, decay_made, emt_made = (sem("m_cast"), sem("arg_made"), sem("decay_made"),
                                              sem("emt_made"))
    ls_done, ls_made, num_done, abs_made, num_made = (sem("ls_done"), sem("ls_made"), sem("num_done"),
                                                      sem("abs_made"), sem("num_made"))
    lsq_made, lss_done, lroot_made, mix_made = (sem("lsq_made"), sem("lss_done"), sem("lroot_made"),
                                                sem("mix_made"))
    out_turned, out_made = sem("out_turned"), sem("out_made")
    act_own, dve_own, pool_own = sem("act_own"), sem("dve_own"), sem("pool_own")

    conv_ready_made = sem("conv_ready_made")
    c_basic, c_block1 = 6, 6 + 21
    c_pad, c_comb, c_dil = c_block1 + 2, c_block1 + 2 + 3, c_block1 + 2 + 3 + 6

    def halves(ap):
        return ap.rearrange("p k (two n) -> p k two n", two=2)

    def pair(bank, n=T):
        return ps[:, bank, 0:2 * n].rearrange("p (a n) -> p a n", a=2)

    def evacs(g):
        return g + 1 - FT * sum(g >= f + FT for f in FFNS)

    def gbank(g):
        return 4 + g % 4

    def token_view(tile):
        return tile[:, :, :].rearrange("p k t -> p (k t)").rearrange("p (a d) -> p a d", a=TT)

    def w1_view(slot):
        return g_raw[:, slot, :, :].rearrange("p k n -> p (k n)").rearrange("p (l n) -> p l n", l=16)

    def par_col(name, i=0, n=1):
        return par[:, ROWS[name] + i:ROWS[name] + i + n]

    def raw_step(g):
        c = CHUNK_OF[g]
        return raw_cols(c % 2, g % 2, CHUNKS[c][0] == "pair")

    def raw_cols(slot, half, paired):
        if paired:
            return halves(g_raw[:, slot, :, :])[:, :, :, half * P:(half + 1) * P]
        return g_raw[:, slot, :, half * 256:(half + 1) * 256]

    def part_view(parts, g, paired):
        return halves(parts[:, g % 2, :, :]) if paired else parts[:, g % 2, :, :]

    def mod_col(i):
        return mod[:, i:i + 1]

    q_t = ybuf
    pct = silu_g
    vrep = hid
    ctmp = e_buf[:, 2, 0:2 * T]
    blk16 = small[:, 0:8]
    cmax = small[:, 16:48]
    q_gain = small[:, 8:9]

    def c4(ap):
        return ap.rearrange("p (x n) -> p x n", n=16)

    A_FILL = {"n0": 0, "n1": 1, "n2": 2, "attn": 3, "n3": 4, "n5": 5, "mix": 6, "n6": 7}

    def piece_ready(eng, n, j):
        if n == 0:
            eng.wait_ge(xres_made, 4)
        elif n in (1, 3, 6):
            eng.wait_ge(g_evac, evacs({1: AO, 3: WO, 6: MO}[n] + j))
        else:
            eng.wait_ge(res_added, {2: 0, 4: 4, 5: 8, 7: 12}[n] + j + 1)

    GAINS = {0: ("a_norm", 0), 1: ("f_norm", 0), 3: ("f_norm", 8), 4: ("final_norm", 0)}
    Y_BASE = {0: 0, 1: 8, 2: 16, 3: 32, 5: 40, 6: 48}
    N_ORD = {0: 0, 1: 1, 2: 2, 3: 3, 4: 4, 5: 5, 6: 6}
    glimit = {1: F0, 2: KV, 3: F1, 4: MX, 5: MO, 6: F2, 7: GTOTAL}[last_stage]
    climit = CHUNK_OF[glimit - 1] + 1

    def released(eng, c):
        if c < 0:
            return
        kind, g = CHUNKS[c]
        if kind == "cmp":
            eng.wait_ge(cmp_hid_done, g + 1)
        else:
            eng.wait_ge(g_hi_made, g + 2)
            eng.wait_ge(g_lo_made, g + 2)

    def weight_of(g):
        if g < BG:
            j = (g - CV) // 2
            return t["a_w_in"][0], t["a_w_in"][0], D + 256 * j, 2 * D + 256 * j
        for first, n, w in ((BG, 4, t["a_w_in"][0]), (AO, 4, t["a_w_out"][0]), (KV, 6, t["w_kv"]),
                            (QG, 4, t["b_w_qg"][0]), (WO, 4, t["b_w_o"][0]),
                            (MX, 14, t["w_in_2"][0]), (MO, 4, t["w_out_2"][0])):
            if first <= g < first + n:
                return w, None, 256 * (g - first), None
        f = [F0 <= g < KV, F1 <= g < MX, F2 <= g].index(True)
        return (*ffn_weights(f), 128 * (g - FFNS[f]), None)

    def ffn_weights(f):
        if f == 2:
            return t["w_gate_2"][0], t["w_up_2"][0]
        return t["f_w_gu"][f][:, 0:FFN], t["f_w_gu"][f][:, FFN:2 * FFN]

    def down_weight(f):
        return t["w_down_2"][0] if f == 2 else t["f_w_down"][f]

    def by_tile(w):
        return w.rearrange("(k p) n -> p k n", p=P)

    block = ctx.enter_context(nc.Block())

    @block.sync
    def _(sp):
        def load_pair(slot, wa, wb, ca, cb):
            v = halves(g_raw[:, slot, :, :])
            sp.dma_start(v[:, :, 0, :], by_tile(wa)[:, :, bass.ds(ca, 256)]).then_inc(g_loaded[slot], 16)
            sp.dma_start(v[:, :, 1, :], by_tile(wb)[:, :, bass.ds(cb, 256)]).then_inc(g_loaded[slot], 16)

        def load_g(c):
            slot = c % 2
            released(sp, c - 2)
            kind, g = CHUNKS[c]
            if kind == "cmp":
                w = t["cmp_w1_v" if g else "cmp_w1_k"].rearrange("(l p) n -> p l n", p=P)
                for l in (0, 8):
                    sp.dma_start(w1_view(slot)[:, l:l + 8, :], w[:, l:l + 8, :]).then_inc(g_loaded[slot], 16)
                return
            wa, wb, ca, cb = weight_of(g)
            if kind == "pair":
                load_pair(slot, wa, wb, ca, ca if cb is None else cb)
                return
            for k in (0, 4):
                sp.dma_start(g_raw[:, slot, k:k + 4, :],
                             by_tile(wa)[:, k:k + 4, ca:ca + 512]).then_inc(g_loaded[slot], 16)

        def load_d(f, c, slot):
            src = down_weight(f).rearrange("(c j p) n -> p c j n", j=2, p=P)
            sp.dma_start(d_raw[:, slot:slot + 1, :, :], src[:, bass.ds(c, 1), :, :]).then_inc(d_loaded[slot], 16)

        def load_ffn(f):
            c0, g0, d0, dc0 = CHUNK_OF[FFNS[f]], FFNS[f], FT * f, FT // 2 * f
            for c in range(3):
                load_g(c0 + c)
                if c == 0 and f > 0:
                    sp.wait_ge(g_done, (WO if f == 1 else MO) + 1)
                if dc0 + c >= 2:
                    sp.wait_ge(d_hi_made, 2 * (dc0 + c - 1))
                    sp.wait_ge(d_lo_made, 2 * (dc0 + c - 1))
                load_d(f, c, (dc0 + c) % 2)
            wa, wb = ffn_weights(f)
            with sp.Fori(0, 4) as i:
                for r in range(2):
                    sp.wait_ge(g_hi_made, i * 4 + (g0 + 4 + 2 * r))
                    sp.wait_ge(g_lo_made, i * 4 + (g0 + 4 + 2 * r))
                    load_pair((c0 + 3 + r) % 2, wa, wb, i * 512 + 256 * (3 + r), i * 512 + 256 * (3 + r))
                    sp.wait_ge(d_hi_made, i * 4 + (d0 + 4 + 2 * r))
                    sp.wait_ge(d_lo_made, i * 4 + (d0 + 4 + 2 * r))
                    load_d(f, i * 2 + (3 + r), (dc0 + 3 + r) % 2)

        c = 0
        while c < climit:
            g = CHUNKS[c][1] if CHUNKS[c][0] != "cmp" else -1
            if g in FFNS:
                load_ffn(FFNS.index(g))
                c += FT // 2
            else:
                load_g(c)
                c += 1
        res = token_view(ybuf)
        dst = out[0].rearrange("(a p) d -> p a d", p=P)
        for q in range(4):
            a, h = q % 2, q // 2
            sp.wait_ge(out_made, q + 1)
            sp.dma_start(dst[:, a, h * 512:(h + 1) * 512], res[:, a, h * 512:(h + 1) * 512]).then_inc(stored, 16)
        sp.wait_ge(stored, 64)

    @block.gpsimd
    def _(pool):
        made = [0]

        def const(ins):
            made[0] += 1
            ins.then_inc(consts, 1)
            pool.wait_ge(consts, made[0])

        const(pool.memset(ident[:, :], 0.0))
        const(pool.affine_select(out=ident[:, :], in_=ident[:, :], compare_op=ALU.not_equal, fill=1.0,
                                 base=0, pattern=[[-1, P]], channel_multiplier=1))
        const(pool.memset(ones[:, :], 1.0))
        const(pool.memset(eps[:, 0:1], 1e-5))
        const(pool.memset(eps[:, 1:2], 1e-6))
        const(pool.memset(zpad[:, :, 0:4], 0.0))
        assert made[0] == c_basic

        w_ada = t["w_ada_2"][0].rearrange("(k p) n -> p k n", p=P)

        def load_ada(m):
            n, k = m // KT, m % KT
            pool.dma_start(ada_raw[:, m % 2, :], w_ada[:, k, n * D:(n + 1) * D]).then_inc(ada_loaded[m % 2], 16)

        load_ada(0)
        load_ada(1)
        const(pool.memset(ones64[:, :], 0.0))
        const(pool.memset(ones64[0:HD, 0:HD], 1.0))
        const(pool.memset(ones64[HD:P, HD:P], 1.0))
        for a, lo, w in ((1, 0, 256), (0, 256, 128)):
            d = dist[:, lo:lo + w]
            const(pool.iota(d, pattern=[[1, w]], base=-P * a, channel_multiplier=-1,
                            allow_small_or_imprecise_dtypes=True))
            const(pool.affine_select(out=d, in_=d, compare_op=ALU.is_ge, fill=NEG, base=P * a,
                                     pattern=[[-1, w]], channel_multiplier=1))
        cd = cmp_bias[:, 0, :, 0, :]
        const(pool.iota(cd, pattern=[[-P, TT], [16, 16]], base=0, channel_multiplier=-1,
                        allow_small_or_imprecise_dtypes=True))
        const(pool.tensor_scalar(cd, cd, 15.5, None, ALU.add))
        const(pool.affine_select(out=cd, in_=cd, compare_op=ALU.is_ge, fill=NEG, base=-31,
                                 pattern=[[P, TT], [-16, 16]], channel_multiplier=1))
        for h in range(NH - 1, -1, -1):
            last = pool.tensor_scalar(cmp_bias[:, h % 2, :, h // 2, :], cd, SLOPES[h], None, ALU.mult)
        const(last)
        const(pool.memset(any_vis[:, :], 1.0))
        const(pool.affine_select(out=any_vis[:, 0:1], in_=any_vis[:, 0:1], compare_op=ALU.is_ge, fill=0.0,
                                 base=-31, pattern=[[0, 1]], channel_multiplier=1))
        const(pool.memset(blk16, 1.0))
        const(pool.affine_select(out=blk16, in_=blk16, compare_op=ALU.is_ge, fill=0.0, base=0,
                                 pattern=[[-16, 8]], channel_multiplier=1))
        const(pool.affine_select(out=blk16, in_=blk16, compare_op=ALU.is_ge, fill=0.0, base=15,
                                 pattern=[[16, 8]], channel_multiplier=-1))
        const(pool.memset(lstm_mask[:, :], 0.0))
        for lo, w in ((0, 256), (256, 128)):
            m = lstm_mask[:, lo:lo + w]
            const(pool.affine_select(out=m, in_=m, compare_op=ALU.is_ge, fill=NEG, base=0,
                                     pattern=[[1, w]], channel_multiplier=-1))
        const(pool.memset(sel4[:, :, :], 0.0))
        const(pool.affine_select(out=sel4[:, :, :], in_=sel4[:, :, :], compare_op=ALU.not_equal, fill=1.0,
                                 base=0, pattern=[[-1, NM], [0, P]], channel_multiplier=1))
        assert made[0] == c_block1

        pool.wait_ge(csil_made, 1)
        for m in range(6 * KT):
            n, k = m // KT, m % KT
            acc = ada_acc[:, n * D:(n + 1) * D]
            pool.wait_ge(ada_loaded[m % 2], 16 * (m // 2 + 1))
            if k == 0:
                ins = pool.tensor_scalar(acc, ada_raw[:, m % 2, :], csil[:, k:k + 1], None, ALU.mult)
            else:
                raw = ada_raw[:, m % 2, :]
                pool.tensor_scalar(raw, raw, csil[:, k:k + 1], None, ALU.mult).then_inc(ada_scaled, 1)
                pool.wait_ge(ada_scaled, m - n)
                ins = pool.tensor_tensor(acc, acc, raw, ALU.add)
            ins.then_inc(ada_added, 1)
            pool.wait_ge(ada_added, m + 1)
            if m + 2 < 6 * KT:
                load_ada(m + 2)

        if last_stage >= 3:
            pool.wait_ge(d_done, FT)
            for w in range(2):
                pool.dma_start(w2_k[:, :, w, :], t["cmp_w2_k"].rearrange("(a p) n -> p a n", p=P)).then_inc(w2_loaded, 16)
            pool.dma_start(w2_v[:, :, :], t["cmp_w2_v"].rearrange("(a p) n -> p a n", p=P)).then_inc(w2_loaded, 16)
            const(pool.memset(x_cmp[:, :, :, 256:288], 0.0))
            const(pool.memset(x_cmp[HD:P, :, :, 255:256], 0.0))
            assert made[0] == c_pad

            def head_bias(h):
                pool.tensor_scalar(bias_h[:, h % 2, :], dist[:, :], SLOPES[h], None, ALU.mult).then_inc(bias_made, 1)

            pool.wait_ge(gate_done, 1)
            head_bias(0)
            head_bias(1)
            for h in range(NH):
                pool.wait_ge(fac_made, h + 1)
                for a, b, lo, w in ((1, 0, 0, 256), (1, 1, 256, 256), (0, 0, 512, 128), (0, 1, 640, 128)):
                    e = e_buf[:, h % 3, lo:lo + w]
                    i = 2 * a + b
                    last = pool.tensor_scalar(e, e, fac[:, h % 3, i:i + 1], None, ALU.mult)
                last.then_inc(scaled, 1)
                if h + 2 < NH:
                    head_bias(h + 2)
        if last_stage >= 5:
            pool.wait_ge(ada_summed, 1)
            const(pool.memset(comb[:, :, :], 0.0))
            for i, r in ((0, 4), (1, 16)):
                v = comb[0:r, i, :].rearrange("p (m j) -> p m j", j=r)
                const(pool.affine_select(out=v, in_=v, compare_op=ALU.not_equal, fill=1.0, base=0,
                                         pattern=[[0, T // r], [-1, r]], channel_multiplier=1))
            assert made[0] == c_comb
            const(pool.memset(dil_mask[:, :], 1.0))
            band = dil_mask[:, 0:256]
            const(pool.affine_select(out=band, in_=band, compare_op=ALU.is_ge, fill=0.0, base=0,
                                     pattern=[[1, 256]], channel_multiplier=-1))
            pool.wait_ge(comb_done, 2)
            const(pool.tensor_tensor(dil_count[:, :], dil_count[:, :], dil_mask[:, :], ALU.add))
            for a, lo, w in ((1, 0, 256), (0, 256, 128)):
                v = dil_count[:, lo:lo + w]
                const(pool.affine_select(out=v, in_=v, compare_op=ALU.is_ge, fill=0.0, base=P * a,
                                         pattern=[[-1, w]], channel_multiplier=1))
            const(pool.tensor_scalar(dil_mask[:, :], dil_count[:, :], 0.5, NEG, ALU.is_lt, ALU.mult))
            assert made[0] == c_dil
        if last_stage >= 6:
            for h in range(NH2):
                pool.wait_ge(fac_made, NH + h + 1)
                for a, lo, w in ((1, 0, 256), (0, 256, 128)):
                    e = e_dil[:, h % 3, lo:lo + w]
                    last = pool.tensor_scalar(e, e, fac[:, h % 3, a:a + 1], None, ALU.mult)
                last.then_inc(scaled, 1)

    @block.scalar
    def _(act):
        def split_g(g):
            if g >= glimit:
                return
            c = CHUNK_OF[g]
            act.wait_ge(g_loaded[c % 2], 32 * (c // 2 + 1))
            if g >= 2:
                act.wait_ge(g_done, g - 1)
            paired = CHUNKS[c][0] == "pair"
            act.activation(part_view(g_hi, g, paired), raw_step(g), ACT.Copy).then_inc(g_hi_made, 1)

        def norm_root(n, fills):
            for j in range(4):
                piece_ready(act, n, j)
                act.activation(ybuf[:, 2 * j:2 * j + 2, :], xres[:, 2 * j:2 * j + 2, :], ACT.Square).then_inc(sq_made, 1)
            act.wait_ge(ss_done, n + 1)
            e = 1 if n >= 5 else 0
            act.activation(rstd[:, :], ps[:, 0, 0:T], ACT.Sqrt, scale=1.0 / D, bias=eps[:, e:e + 1]).then_inc(rms_made, 1)
            for buf, signal, y0, bias in fills:
                for k in range(KT):
                    act.wait_ge(y_made, y0 + k + 1)
                    if bias is None:
                        act.activation(buf[:, k, :], ybuf[:, k, :], ACT.Copy).then_inc(signal, 1)
                    else:
                        act.activation(buf[:, k, :], ybuf[:, k, :], ACT.Identity, bias=mod_col(bias + k)).then_inc(signal, 1)

        def split_d(dslot, slot, loaded, free, j):
            act.wait_ge(d_loaded[slot], loaded)
            if free is not None:
                act.wait_ge(d_done, free)
            act.activation(d_hi[:, dslot, :], d_raw[:, slot, j, :], ACT.Copy).then_inc(d_hi_made, 1)

        def ffn(f):
            g0, d0, c0, dc0 = FFNS[f], FT * f, CHUNK_OF[FFNS[f]], FT // 2 * f

            def step(i, r, tail=False, first=False):
                s4 = i * 4
                act.wait_ge(g_done, s4 + (g0 + r + 1))
                act.activation(silu_g[:, r % 2, :], ps[:, gbank(g0 + r), 0:T], ACT.Silu).then_inc(silu_made, 1)
                if tail:
                    split_g(g0 + 20 + r + 2)
                else:
                    c = c0 + (r + 2) // 2
                    act.wait_ge(g_loaded[c % 2], i * 32 + 32 * (c // 2 + 1))
                    act.activation(part_view(g_hi, g0 + r, True), raw_cols(c % 2, r % 2, True),
                                   ACT.Copy).then_inc(g_hi_made, 1)
                act.wait_ge(hid_made, s4 + (d0 + r + 1))
                if not first or d0 + r >= 2:
                    act.wait_ge(d_done, s4 + (d0 + r - 1))
                act.activation(hid_hi[:, r % 2, :], hid[:, r % 2, :], ACT.Copy).then_inc(hid_hi_made, 1)
                if not (tail and r == 1):
                    c = dc0 + (r + 1) // 2
                    free = None if first and d0 + r == 0 else s4 + (d0 + r)
                    split_d((r + 1) % 2, c % 2, i * 16 + 16 * (c // 2 + 1), free, (r + 1) % 2)

            split_d(0, dc0 % 2, 16 * (dc0 // 2 + 1), None, 0)
            norm_root({0: 1, 1: 3, 2: 6}[f],
                      [(opa_hi, opa_hi_made, Y_BASE[{0: 1, 1: 3, 2: 6}[f]], 24 if f == 2 else None)])
            for r in range(4):
                step(0, r, first=True)
            with act.Fori(1, 5) as i:
                for r in range(4):
                    step(i, r)
            for r in range(2):
                step(5, r, tail=True)

        act.dma_start(token_view(ybuf), t["x"][0].rearrange("(a p) d -> p a d", p=P)).then_inc(x_loaded, 16)
        for name, n in (("a_norm", 8), ("kv_norm", 8), ("b_norm", 8), ("f_norm", 16), ("final_norm", 8),
                        ("g_mix_2", 8), ("g_ffn_2", 8), ("c_2", 8), ("a_conv", 24), ("w_conv_2", 32),
                        ("b_conv_2", 8), ("b_ada_2", 48), ("mlstm_norm_g_2", 4)):
            src = t[name]
            if len(src.shape) == 3:
                src = src.rearrange("a j (k p) -> (a j k) p", p=P)
            elif len(src.shape) == 2:
                src = src.rearrange("a (k p) -> (a k) p", p=P)
            else:
                src = src.rearrange("(k p) -> k p", p=P)
            r0, half = ROWS[name] % P, ROWS[name] // P
            act.dma_start(prow[r0:r0 + n, half, :], src).then_inc(par_loaded, 16)
        for name in ("cmp_pe_k", "cmp_pe_v"):
            r0 = ROWS[name] - P
            act.dma_start(prow[r0:r0 + 16, 1, :], t[name].rearrange("(l two) d -> l (two d)", two=2)).then_inc(par_loaded, 16)
        for name in ("q_norm_g_2", "k_norm_g_2"):
            r0 = ROWS[name] - P
            for lo in (0, HD):
                act.dma_start(prow[r0:r0 + 1, 1, lo:lo + HD], t[name]).then_inc(par_loaded, 16)
        act.dma_start(qg_raw[:, :, :], by_tile(t["b_w_qg"][0])[:, :, D:D + 48]).then_inc(side_loaded, 16)
        act.dma_start(if_raw[:, :, :], by_tile(t["w_in_2"][0])[:, :, 3584:3592]).then_inc(side_loaded, 16)
        act.dma_start(if_bias[:, 0:4], t["b_igate_2"].to_broadcast([P, 4])).then_inc(side_loaded, 16)
        act.dma_start(if_bias[:, 4:8], t["b_fgate_2"].to_broadcast([P, 4])).then_inc(side_loaded, 16)
        act.wait_ge(consts, c_basic)
        split_g(0)
        split_g(1)
        act.wait_ge(side_loaded, 64)
        act.activation(qg_hi[:, :, :], qg_raw[:, :, :], ACT.Copy).then_inc(side_hi, 1)
        act.activation(if_hi[:, :, :], if_raw[:, :, :], ACT.Copy).then_inc(side_hi, 1)

        norm_root(0, [(opa_hi, opa_hi_made, 0, None)])
        act.wait_ge(par_made, 1)
        act.activation(csil[:, :], par_col("c_2", 0, 8), ACT.Silu).then_inc(csil_made, 1)
        for i in range(8):
            act.wait_ge(g_done, CV + i + 1)
            if i >= 2:
                act.wait_ge(g_evac, i - 1)
            act.activation(silu_g[:, i % 2, :], ps[:, gbank(CV + i), 0:T], ACT.Copy).then_inc(c_copied, 1)
            split_g(CV + i + 2)
        for s in range(4):
            split_g(BG + s + 2)
            act.wait_ge(g_evac, BG + s + 1)
            act.activation(opb_hi[:, 2 * s:2 * s + 2, :], ybuf[:, 2 * s:2 * s + 2, :], ACT.Copy).then_inc(opb_hi_made, 1)
        for s in range(4):
            split_g(AO + s + 2)
        if last_stage >= 2:
            ffn(0)

        if last_stage >= 3:
            norm_root(2, [(opa_hi, opa_hi_made, Y_BASE[2], None), (opb_hi, opb_hi_made, Y_BASE[2] + 8, None)])
            for s in range(6):
                act.wait_ge(g_done, KV + s + 1)
                tiles = pair(gbank(KV + s))
                if s < 2:
                    act.wait_ge(consts, c_pad)
                    x = x_cmp[:, s, :, :].rearrange("p (t two) n -> p t two n", two=2)
                    act.activation(x[0:HD, :, 0, 0:T], tiles[0:HD], ACT.Copy)
                    act.activation(x[HD:P, :, 0, 0:T - 1], tiles[0:HD, :, 1:T], ACT.Copy).then_inc(kv_copied, 1)
                elif s in (2, 4):
                    k = k_dup[:, (s - 2) // 2, :, :].rearrange("p (t two) n -> p t two n", two=2)
                    act.activation(k[0:HD, :, 0, :], tiles[0:HD], ACT.Copy)
                    act.activation(k[HD:P, :, 0, :], tiles[0:HD], ACT.Copy).then_inc(kv_copied, 1)
                split_g(KV + s + 2)
            act.wait_ge(cmp_hid_done, 1)
            act.activation(hid_cmp[:, 0, :, :, :].rearrange("p a g n -> p (a g n)"), ps[:, 0, 0:128],
                           ACT.Silu).then_inc(cmp_hid_silu, 1)
            act.wait_ge(cmp_hid_done, 2)
            for a in range(2):
                src = ps[:, 1, a * 64:(a + 1) * 64].rearrange("p (g n) -> p g n", g=NG)
                act.activation(vrep[:, a, 0:P].rearrange("p (g h n) -> p g h n", g=NG, h=2),
                               src.unsqueeze(2).to_broadcast([P, NG, 2, 16]), ACT.Silu).then_inc(cmp_hid_silu, 1)
            for s in range(4):
                act.wait_ge(g_done, QG + s + 1)
                split_g(QG + s + 2)
            act.wait_ge(gate_done, 1)
            act.activation(gates[:, :, :].rearrange("p a n -> p (a n)"), ps[:, 3, 256:352], ACT.Exp,
                           scale=-1.0).then_inc(gate_exp, 1)
            act.wait_ge(cs_shift, 1)
            act.activation(ctmp, ctmp, ACT.Exp).then_inc(cs_exp, 1)
            act.wait_ge(pct_done, 1)
            act.activation(pct[:, :, :].rearrange("p a n -> p (a n)"), ps[:, 7, :], ACT.Copy).then_inc(pct_made, 1)
            for h in range(NH + 2):
                if h < NH:
                    act.wait_ge(shifted, h + 1)
                    for a, b, lo, w in ((1, 0, 0, 256), (1, 1, 256, 256), (0, 0, 512, 128), (0, 1, 640, 128)):
                        e = e_buf[:, h % 3, lo:lo + w]
                        i = 2 * a + b
                        last = act.activation(e, e, ACT.Exp, bias=nmax[:, h % 3, i:i + 1], scale=-1.0,
                                              accum_out=zsum[:, h % 3, i:i + 1])
                    last.then_inc(exp_made, 1)
                if h >= 2:
                    act.wait_ge(pt_done, h - 1)
                    act.activation(pt_buf[:, 0, :], ps[:, 4, 0:384], ACT.Copy).then_inc(pt_slc, 1)
                if h >= 3 and h % 2 == 1:
                    j = (h - 3) // 2
                    act.wait_ge(pv_done, 2 * j + 2)
                    act.activation(opa_hi[:, j, :], ps[:, 6 + j % 2, 0:T], ACT.Copy).then_inc(opa_hi_made, 1)
            for s in range(4):
                act.wait_ge(g_done, WO + s + 1)
                split_g(WO + s + 2)
        if last_stage >= 4:
            ffn(1)

        if last_stage >= 5:
            norm_root(4, [])
            norm_root(5, [(opa_hi, opa_hi_made, Y_BASE[5], 0)])
            for s in range(14):
                g = MX + s
                act.wait_ge(g_done, g + 1)
                if MX_QM <= g < MX_VM:
                    n = g - MX_QM
                    if n >= 1:
                        act.wait_ge(conv_made, n)
                    act.activation(zpad[:, :, 4:T + 4], pair(gbank(g)), ACT.Copy).then_inc(z_copied, 1)
                split_g(g + 2)
                if MX_QM <= g < MX_VM:
                    act.wait_ge(conv_made, n + 1)
                    m = qk_m[:, 2 * n:2 * n + 2, :]
                    act.activation(m, m, ACT.Silu).then_inc(conv_ready_made, 1)
                if g >= MX_OG:
                    n = g - MX_OG
                    act.activation(og_s[:, 2 * n:2 * n + 2, :], pair(gbank(g)), ACT.Exp, scale=-1.0).then_inc(og_exp, 1)

        if last_stage >= 6:
            for j in range(4):
                act.wait_ge(g_evac, evacs(MX + j))
                act.activation(ybuf[:, 2 * j:2 * j + 2, :], qk_a[:, 2 * j:2 * j + 2, :], ACT.Square).then_inc(qk_sq, 1)
            for j in range(4):
                act.wait_ge(qk_ss, j + 1)
                act.activation(ybuf[:, 2 * j:2 * j + 2, :], pair(j), ACT.Sqrt, scale=1.0 / HD,
                               bias=eps[:, 1:2]).then_inc(qk_root, 1)
            act.wait_ge(if_in, 1)
            act.activation(if_tmp[:, :, 0, :], if_tok[:, :, 4:8], ACT.Abs).then_inc(act_own, 1)
            act.wait_ge(act_own, 1)
            act.activation(if_tmp[:, :, 1, :], if_tmp[:, :, 0, :], ACT.Exp, scale=-1.0).then_inc(act_own, 1)
            act.wait_ge(act_own, 2)
            act.activation(if_tmp[:, :, 2, :], if_tmp[:, :, 1, :], ACT.Ln, bias=1.0).then_inc(if_abs, 1)
            for h in range(NH2 + 2):
                if h < NH2:
                    act.wait_ge(shifted, NH + h + 1)
                    for a, lo, w in ((1, 0, 256), (0, 256, 128)):
                        e = e_dil[:, h % 3, lo:lo + w]
                        last = act.activation(e, e, ACT.Exp, bias=nmax[:, h % 3, a:a + 1], scale=-1.0)
                    last.then_inc(exp_made, 1)
                if h >= 2:
                    act.wait_ge(pt_done, NH + h - 1)
                    act.activation(pt_dil[:, h % 2, :], ps[:, 4 + h % 2, 0:384], ACT.Copy).then_inc(pt_slc, 1)
                if h >= 3 and h % 2 == 1:
                    j = (h - 3) // 2
                    act.wait_ge(pv_done, NH + 2 * j + 2)
                    act.activation(opa_hi[:, j, :], ps[:, 6 + j % 2, 0:T], ACT.Copy).then_inc(opa_hi_made, 1)
            for m in range(NM):
                b = m % 2
                if m >= 2:
                    act.wait_ge(num_made, m - 1)
                act.wait_ge(arg_made, m + 1)
                act.activation(l_emt[:, b, :], ps[:, b, T:2 * T], ACT.Exp, scale=-1.0).then_inc(emt_made, 1)
                act.activation(decay[:, b, 0:256], decay[:, b, 0:256], ACT.Exp, bias=a_col[:, 0, m:m + 1])
                act.activation(decay[:, b, 256:384], decay[:, b, 256:384], ACT.Exp,
                               bias=a_col[:, 1, m:m + 1]).then_inc(decay_made, 1)
                act.wait_ge(num_done, m + 1)
                act.activation(l_abs[:, b, :], ps[:, 4 + b, T:2 * T], ACT.Abs).then_inc(abs_made, 1)
                act.wait_ge(num_made, m + 1)
                act.activation(l_sq[:, b, :], mix[:, 4 + m, :], ACT.Square).then_inc(lsq_made, 1)
            for j in range(2):
                act.wait_ge(lss_done, 2 * j + 2)
                act.activation(mix[:, 2 * j:2 * j + 2, :], pair(6 + j), ACT.Sqrt, scale=1.0 / P,
                               bias=eps[:, 1:2]).then_inc(lroot_made, 1)
            for m in range(NM):
                act.wait_ge(mix_made, m + 1)
                act.activation(opa_hi[:, 4 + m, :], mix[:, 4 + m, :], ACT.Copy).then_inc(opa_hi_made, 1)
            for s in range(4):
                act.wait_ge(g_done, MO + s + 1)
                split_g(MO + s + 2)
        if last_stage >= 7:
            ffn(2)

    @block.vector
    def _(dve):
        links = [0]

        def own(ins):
            links[0] += 1
            ins.then_inc(dve_own, 1)
            dve.wait_ge(dve_own, links[0])

        def split_g(g):
            if g >= glimit:
                return
            paired = CHUNKS[CHUNK_OF[g]][0] == "pair"
            dve.wait_ge(g_hi_made, g + 1)
            dve.tensor_tensor(part_view(g_lo, g, paired), raw_step(g), part_view(g_hi, g, paired).bitcast(F32),
                              ALU.subtract).then_inc(g_lo_made, 1)

        def norm_parts(n, fills):
            dve.wait_ge(rms_made, n + 1)
            own(dve.reciprocal(rstd[:, :], rstd[:, :]))
            for hi, lo, hi_signal, hi0, lo_signal, gain, bias in fills:
                def make_y(k):
                    dve.scalar_tensor_tensor(out=ybuf[:, k, :], in0=xres[:, k, :], scalar=gain(k), in1=rstd[:, :],
                                             op0=ALU.mult, op1=ALU.mult).then_inc(y_made, 1)
                make_y(0)
                make_y(1)
                for k in range(KT):
                    if k + 2 < KT:
                        make_y(k + 2)
                    dve.wait_ge(hi_signal, hi0 + k + 1)
                    h = hi[:, k, :].bitcast(F32)
                    if bias is None:
                        ins = dve.tensor_tensor(lo[:, k, :], ybuf[:, k, :], h, ALU.subtract)
                    else:
                        ins = dve.scalar_tensor_tensor(out=lo[:, k, :], in0=ybuf[:, k, :], scalar=mod_col(bias + k),
                                                       in1=h, op0=ALU.add, op1=ALU.subtract)
                    ins.then_inc(lo_signal, 1)

        def gain_of(name, first=0):
            return lambda k: par_col(name, first + k)

        def fill_a(fill, gain, bias=None):
            return (opa_hi, opa_lo, opa_hi_made, 8 * A_FILL[fill], opa_made, gain, bias)

        def split_d(dslot, slot, n, j):
            dve.wait_ge(d_hi_made, n)
            dve.tensor_tensor(d_lo[:, dslot, :], d_raw[:, slot, j, :], d_hi[:, dslot, :].bitcast(F32),
                              ALU.subtract).then_inc(d_lo_made, 1)

        def ffn(f, norm, fill, gain, bias):
            g0, d0, c0, dc0 = FFNS[f], FT * f, CHUNK_OF[FFNS[f]], FT // 2 * f

            def step(i, r, tail):
                s4 = i * 4
                dve.wait_ge(silu_made, s4 + (d0 + r + 1))
                dve.tensor_tensor(hid[:, r % 2, :], silu_g[:, r % 2, :], ps[:, gbank(g0 + r), T:2 * T],
                                  ALU.mult).then_inc(hid_made, 1)
                if tail:
                    split_g(g0 + 20 + r + 2)
                else:
                    c = c0 + (r + 2) // 2
                    dve.wait_ge(g_hi_made, s4 + (g0 + r + 3))
                    dve.tensor_tensor(part_view(g_lo, g0 + r, True), raw_cols(c % 2, r % 2, True),
                                      part_view(g_hi, g0 + r, True).bitcast(F32), ALU.subtract).then_inc(g_lo_made, 1)
                dve.wait_ge(hid_hi_made, s4 + (d0 + r + 1))
                dve.tensor_tensor(hid_lo[:, r % 2, :], hid[:, r % 2, :], hid_hi[:, r % 2, :].bitcast(F32),
                                  ALU.subtract).then_inc(hid_lo_made, 1)
                if not (tail and r == 1):
                    c = dc0 + (r + 1) // 2
                    split_d((r + 1) % 2, c % 2, s4 + (d0 + r + 2), (r + 1) % 2)

            split_d(0, dc0 % 2, d0 + 1, 0)
            norm_parts(norm, [fill_a(fill, gain, bias)])
            if f == 1:
                dve.wait_ge(ada_summed, 1)
                own(dve.tensor_tensor(mod[:, :], ps[:, 1, 0:48], par_col("b_ada_2", 0, 48), ALU.add))
                dve.scalar_tensor_tensor(out=gmod[:, 0:8], in0=mod[:, 8:16], scalar=1.0, in1=par_col("g_mix_2", 0, 8),
                                         op0=ALU.add, op1=ALU.mult).then_inc(mod_made, 1)
                dve.scalar_tensor_tensor(out=gmod[:, 8:16], in0=mod[:, 32:40], scalar=1.0, in1=par_col("g_ffn_2", 0, 8),
                                         op0=ALU.add, op1=ALU.mult).then_inc(mod_made, 1)
                dve.wait_ge(mod_made, 2)
                own(dve.tensor_scalar(q_gain, par_col("q_norm_g_2"), HD ** -0.5, None, ALU.mult))
            with dve.Fori(0, 5) as i:
                for r in range(4):
                    step(i, r, False)
            for r in range(2):
                step(5, r, True)
            dve.wait_ge(d_done, d0 + FT)
            for j in range(4):
                if f < 2:
                    x = xres[:, 2 * j:2 * j + 2, :]
                    dve.tensor_tensor(x, pair(j), x, ALU.add).then_inc(res_added, 1)
                    continue
                for k in (2 * j, 2 * j + 1):
                    ins = dve.scalar_tensor_tensor(out=xres[:, k, :], in0=pair(j)[:, k % 2, :], scalar=mod_col(40 + k),
                                                   in1=xres[:, k, :], op0=ALU.mult, op1=ALU.add)
                ins.then_inc(res_added, 1)

        def evac(ins, g):
            ins.then_inc(g_evac, 1)
            dve.wait_ge(g_evac, evacs(g))

        for j in range(4):
            dve.wait_ge(x_turned, j + 1)
            dve.tensor_copy(xres[:, 2 * j:2 * j + 2, :], pair(j)).then_inc(xres_made, 1)
        dve.wait_ge(par_turned, 1)
        dve.tensor_copy(par[:, :], ps[:, 4, 0:NROWS]).then_inc(par_made, 1)
        dve.wait_ge(par_made, 1)
        split_g(0)
        split_g(1)
        for n, (hi, lo, raw) in enumerate(((qg_hi, qg_lo, qg_raw), (if_hi, if_lo, if_raw))):
            dve.wait_ge(side_hi, n + 1)
            dve.tensor_tensor(lo[:, :, :], raw[:, :, :], hi[:, :, :].bitcast(F32), ALU.subtract).then_inc(side_lo, 1)

        norm_parts(0, [fill_a("n0", gain_of("a_norm"))])
        for i in range(8):
            g = CV + i
            dve.wait_ge(c_copied, i + 1)
            z, u = zpad[:, i % 2, :], ybuf[:, i, :]
            evac(dve.tensor_tensor(z[:, 4:T + 4], ps[:, gbank(g), T:2 * T], silu_g[:, i % 2, :], ALU.mult), g)
            own(dve.tensor_scalar(u, z[:, 2:T + 2], par_col("a_conv", i), None, ALU.mult))
            for w in (1, 2):
                own(dve.scalar_tensor_tensor(out=u, in0=z[:, 2 + w:T + 2 + w], scalar=par_col("a_conv", 8 * w + i),
                                             in1=u, op0=ALU.mult, op1=ALU.add))
            split_g(g + 2)
        for s in range(4):
            y = ybuf[:, 2 * s:2 * s + 2, :]
            dve.wait_ge(g_done, BG + s + 1)
            evac(dve.tensor_tensor(y, pair(gbank(BG + s)), y, ALU.mult), BG + s)
            split_g(BG + s + 2)
            dve.wait_ge(opb_hi_made, s + 1)
            dve.tensor_tensor(opb_lo[:, 2 * s:2 * s + 2, :], y, opb_hi[:, 2 * s:2 * s + 2, :].bitcast(F32),
                              ALU.subtract).then_inc(opb_made, 1)

        def add_product(first):
            for s in range(4):
                dve.wait_ge(g_done, first + s + 1)
                x = xres[:, 2 * s:2 * s + 2, :]
                evac(dve.tensor_tensor(x, pair(gbank(first + s)), x, ALU.add), first + s)
                split_g(first + s + 2)

        add_product(AO)
        if last_stage >= 2:
            ffn(0, 1, "n1", gain_of("f_norm"), None)

        if last_stage >= 3:
            norm_parts(2, [fill_a("n2", gain_of("kv_norm")),
                           (opb_hi, opb_lo, opb_hi_made, 4, opb_made, gain_of("b_norm"), None)])

            def cmp_blocks(w):
                pe = par_col("cmp_pe_v" if w else "cmp_pe_k", 0, 16)
                for q in range(2):
                    x = x_cmp[:, w, :, 16 * q:16 * q + 256].rearrange("p g (n l two) -> p l g n two", l=8, two=2)
                    e = pe[:, 8 * q:8 * q + 8].unsqueeze(2).unsqueeze(3).to_broadcast([P, 8, NG, 16])
                    dve.tensor_tensor(b_cmp[:, 8 * q:8 * q + 8, :, :], x[:, :, :, :, 0], e, ALU.add).then_inc(b_cmp_made, 1)

            for s in range(6):
                g = KV + s
                dve.wait_ge(g_done, g + 1)
                tiles = pair(gbank(g))
                if s < 2:
                    dve.wait_ge(consts, c_pad)
                    x = x_cmp[:, s, :, :].rearrange("p (t two) n -> p t two n", two=2)
                    dve.tensor_copy(x[0:HD, :, 1, 0:T], tiles[HD:P])
                    dve.wait_ge(kv_copied, s + 1)
                    evac(dve.tensor_copy(x[HD:P, :, 1, 0:T - 1], tiles[HD:P, :, 1:T]), g)
                    if s == 0:
                        cmp_blocks(0)
                elif s in (2, 4):
                    k = k_dup[:, (s - 2) // 2, :, :].rearrange("p (t two) n -> p t two n", two=2)
                    dve.tensor_copy(k[0:HD, :, 1, :], tiles[HD:P])
                    dve.wait_ge(kv_copied, 2 + s // 2)
                    evac(dve.tensor_copy(k[HD:P, :, 1, :], tiles[HD:P]), g)
                else:
                    evac(dve.tensor_copy(v_tok[:, (s - 3) // 2, :, :], tiles), g)
                if s == 5:
                    dve.wait_ge(cmp_hid_done, 1)
                    cmp_blocks(1)
                split_g(g + 2)
            for s in range(4):
                g = QG + s
                dve.wait_ge(g_done, g + 1)
                evac(dve.tensor_scalar(q_t[:, 2 * s:2 * s + 2, :], pair(gbank(g)), HD ** -0.5, None, ALU.mult), g)
                split_g(g + 2)
            dve.wait_ge(gate_exp, 1)
            own(dve.tensor_scalar(gates[:, :, :], gates[:, :, :], 1.0, None, ALU.add))
            dve.reciprocal(gates[:, :, :], gates[:, :, :]).then_inc(gates_made, 1)
            dve.wait_ge(kc_done, 1)
            dve.wait_ge(consts, c_block1)
            dve.tensor_copy(kc_dup[:, :, :].rearrange("p g n -> p (g n)"), ps[:, 2, 0:64]).then_inc(kc_made, 1)
            v = ps[:, 2, 64:128].unsqueeze(1).to_broadcast([P, 8, HD])
            dve.tensor_tensor(vc_blk[:, :, :], v, blk16.unsqueeze(2).to_broadcast([P, 8, HD]),
                              ALU.mult).then_inc(kc_made, 1)
            dve.wait_ge(cs_done, 1)
            own(dve.tensor_tensor(ctmp.rearrange("p (b x) -> p b x", b=2), ps[:, 0:2, 0:T],
                                  cmp_bias[:, :, :, :, :].rearrange("p b a h n -> p b (a h n)"), ALU.add))
            own(dve.tensor_reduce(cmax, c4(ctmp), AX_X, ALU.max))
            dve.tensor_tensor(c4(ctmp), c4(ctmp), cmax.unsqueeze(2).to_broadcast([P, 32, 16]),
                              ALU.subtract).then_inc(cs_shift, 1)
            dve.wait_ge(cs_exp, 1)
            own(dve.tensor_reduce(cmax, c4(ctmp), AX_X, ALU.add))
            own(dve.reciprocal(cmax, cmax))
            dve.wait_ge(gates_made, 1)
            gate0 = gates[:, :, :].rearrange("p a (h two b) -> p two a h b", two=2, b=3)[:, :, :, :, 0]
            c = cmax.rearrange("p (b a h) -> p b a h", b=2, a=TT)
            for b in range(2):
                last = dve.tensor_tensor(cfac[:, b, :, :], c[:, b, :, :], gate0[:, b, :, :], ALU.mult)
            own(last)
            own(dve.tensor_tensor(cfac[:, :, :, :], cfac[:, :, :, :],
                                  any_vis[:, :].unsqueeze(1).unsqueeze(3).to_broadcast([P, 2, TT, 8]), ALU.mult))
            f = cfac[:, :, :, :].rearrange("p b a h -> p (b a h)")
            dve.tensor_tensor(c4(ctmp), c4(ctmp), f.unsqueeze(2).to_broadcast([P, 32, 16]), ALU.mult).then_inc(cs_made, 1)
            for h in range(NH + 2):
                if h < NH:
                    dve.wait_ge(scored, h + 1)
                    dve.wait_ge(bias_made, h + 1)
                    for a, b, lo, w in ((1, 0, 0, 256), (1, 1, 256, 256), (0, 0, 512, 128), (0, 1, 640, 128)):
                        i = 2 * a + b
                        src = ps[:, 2 * (h % 2) + (1 - a), b * w:(b + 1) * w]
                        bias = bias_h[:, h % 2, 0:256] if a else bias_h[:, h % 2, 256:384]
                        last = dve.tensor_tensor_reduce(e_buf[:, h % 3, lo:lo + w], src, bias, -1.0, 3.0e38,
                                                        ALU.add, ALU.min, nmax[:, h % 3, i:i + 1])
                    last.then_inc(shifted, 1)
                if 1 <= h <= NH:
                    p = h - 1
                    dve.wait_ge(exp_made, p + 1)
                    own(dve.reciprocal(fac[:, p % 3, :], zsum[:, p % 3, :]))
                    g2 = gates[:, :, 3 * p + 1:3 * p + 3]
                    f4 = fac[:, p % 3, :].rearrange("p (a b) -> p a b", a=TT)
                    dve.tensor_tensor(f4, f4, g2, ALU.mult).then_inc(fac_made, 1)
                if h >= 2:
                    dve.wait_ge(pt_done, h - 1)
                    dve.tensor_copy(pt_buf[:, 1, :], ps[:, 5, 0:384]).then_inc(pt_win, 1)
                if h >= 3 and h % 2 == 1:
                    j = (h - 3) // 2
                    dve.wait_ge(opa_hi_made, 8 * A_FILL["attn"] + j + 1)
                    dve.tensor_tensor(opa_lo[:, j, :], ps[:, 6 + j % 2, 0:T], opa_hi[:, j, :].bitcast(F32),
                                      ALU.subtract).then_inc(opa_made, 1)
            add_product(WO)
        if last_stage >= 4:
            ffn(1, 3, "n3", gain_of("f_norm", 8), None)

        if last_stage >= 5:
            dve.wait_ge(rms_made, 5)
            own(dve.reciprocal(rstd[:, :], rstd[:, :]))
            for k in range(KT):
                ins = dve.scalar_tensor_tensor(out=xres[:, k, :], in0=xres[:, k, :], scalar=par_col("final_norm", k),
                                               in1=rstd[:, :], op0=ALU.mult, op1=ALU.mult)
                if k % 2 == 1:
                    ins.then_inc(res_added, 1)
            dve.wait_ge(comb_done, 1)
            dve.tensor_copy(dil_count[:, :], ps[:, 1, 0:384]).then_inc(comb_done, 1)
            norm_parts(5, [fill_a("n5", lambda k: gmod[:, k:k + 1], 0)])
            for s in range(14):
                g = MX + s
                dve.wait_ge(g_done, g + 1)
                tiles = pair(gbank(g))
                if g < MX_VA:
                    evac(dve.tensor_copy(qk_a[:, 2 * s:2 * s + 2, :], tiles), g)
                elif g < MX_QM:
                    n = g - MX_VA
                    evac(dve.tensor_copy(v_a[:, :, n * T:(n + 1) * T], tiles), g)
                elif g < MX_VM:
                    n = g - MX_QM
                    dve.wait_ge(z_copied, n + 1)
                    for a in range(2):
                        i, z = 2 * n + a, zpad[:, a, :]
                        u = qk_m[:, i, :]
                        ins = dve.tensor_scalar(u, z[:, 1:T + 1], par_col("w_conv_2", i), par_col("b_conv_2", i),
                                                ALU.mult, ALU.add)
                        if a == 0:
                            evac(ins, g)
                        else:
                            own(ins)
                        for w in (1, 2, 3):
                            ins = dve.scalar_tensor_tensor(out=u, in0=z[:, 1 + w:T + 1 + w],
                                                           scalar=par_col("w_conv_2", 8 * w + i), in1=u,
                                                           op0=ALU.mult, op1=ALU.add)
                            if w < 3:
                                own(ins)
                    ins.then_inc(conv_made, 1)
                elif g < MX_OG:
                    n = g - MX_VM
                    evac(dve.tensor_copy(v_m[:, :, n * T:(n + 1) * T], tiles), g)
                else:
                    n = g - MX_OG
                    o = og_s[:, 2 * n:2 * n + 2, :]
                    dve.wait_ge(og_exp, n + 1)
                    evac(dve.tensor_scalar(o, o, 1.0, None, ALU.add), g)
                    own(dve.reciprocal(o, o))
                split_g(g + 2)

        if last_stage >= 6:
            dve.wait_ge(if_done, 1)
            dve.wait_ge(side_loaded, 64)
            dve.tensor_tensor(if_tok[:, :, :], ps[:, 4, 0:16].rearrange("p (a n) -> p a n", a=TT),
                              if_bias[:, :].unsqueeze(1).to_broadcast([P, TT, 8]), ALU.add).then_inc(if_in, 1)
            for j in range(4):
                dve.wait_ge(qk_root, j + 1)
                own(dve.reciprocal(ybuf[:, 2 * j:2 * j + 2, :], ybuf[:, 2 * j:2 * j + 2, :]))
                for k in (2 * j, 2 * j + 1):
                    ins = dve.scalar_tensor_tensor(out=qk_a[:, k, :], in0=qk_a[:, k, :],
                                                   scalar=q_gain if k < 4 else par_col("k_norm_g_2"),
                                                   in1=ybuf[:, k, :], op0=ALU.mult, op1=ALU.mult)
                ins.then_inc(qk_made, 1)
            dve.wait_ge(if_abs, 1)
            dve.scalar_tensor_tensor(out=if_tok[:, :, 4:8], in0=if_tok[:, :, 4:8], scalar=0.0, in1=if_tmp[:, :, 2, :],
                                     op0=ALU.min, op1=ALU.subtract).then_inc(if_tok_made, 1)
            dve.wait_ge(rows_turned, 1)
            own(dve.memset(ones_row[:, :], 1.0))
            own(dve.tensor_copy(rows[:, 0:2, :], ps[0:NM, 5, :].rearrange("p (a n) -> p a n", a=2)))
            own(dve.tensor_tensor_scan(rows[:, 2, :], ones_row[:, :], rows[:, 1, :], 0.0, ALU.mult, ALU.add))
            own(dve.tensor_tensor(rows[:, 3, :], rows[:, 0, :], rows[:, 2, :], ALU.subtract))
            own(dve.tensor_tensor_scan(rows[:, 4, :], ones_row[:, :], rows[:, 3, :], 0.0, ALU.mult, ALU.max))
            dve.tensor_scalar(rows[:, 5, :], rows[:, 4, :], -1.0, None, ALU.mult)
            dve.tensor_tensor(rows[:, 6, :], rows[:, 2, :], rows[:, 4, :], ALU.add).then_inc(rows_made, 1)
            dve.wait_ge(a_turned, 1)
            dve.tensor_copy(a_col[:, :, :], ps[:, 4, 16:24].rearrange("p (a n) -> p a n", a=TT)).then_inc(a_made, 1)
            for h in range(NH2 + 2):
                if h < NH2:
                    dve.wait_ge(scored, NH + h + 1)
                    dve.wait_ge(consts, c_dil)
                    for a, lo, w in ((1, 0, 256), (0, 256, 128)):
                        last = dve.tensor_tensor_reduce(e_dil[:, h % 3, lo:lo + w], ps[:, h % 2, lo:lo + w],
                                                        dil_mask[:, lo:lo + w], -1.0, 3.0e38, ALU.add, ALU.min,
                                                        nmax[:, h % 3, a:a + 1])
                    last.then_inc(shifted, 1)
                if 1 <= h <= NH2:
                    p = h - 1
                    dve.wait_ge(exp_made, NH + p + 1)
                    for a, lo, w in ((1, 0, 256), (0, 256, 128)):
                        e = e_dil[:, p % 3, lo:lo + w]
                        last = dve.tensor_tensor_reduce(e, e, dil_count[:, lo:lo + w], 1.0, 0.0, ALU.mult, ALU.add,
                                                        zsum[:, p % 3, a:a + 1])
                    own(last)
                    dve.reciprocal(fac[:, p % 3, 0:2], zsum[:, p % 3, 0:2]).then_inc(fac_made, 1)
                if h >= 3 and h % 2 == 1:
                    j = (h - 3) // 2
                    dve.wait_ge(opa_hi_made, 8 * A_FILL["mix"] + j + 1)
                    dve.tensor_tensor(opa_lo[:, j, :], ps[:, 6 + j % 2, 0:T], opa_hi[:, j, :].bitcast(F32),
                                      ALU.subtract).then_inc(opa_made, 1)
            for m in range(NM):
                b = m % 2
                dve.wait_ge(m_cast, m + 1)
                dve.tensor_tensor(decay[:, b, 0:256], ps[:, b, 0:T], lstm_mask[:, 0:256], ALU.add)
                dve.tensor_tensor(decay[:, b, 256:384], ps[:, b, P:T], lstm_mask[:, 256:384], ALU.add).then_inc(arg_made, 1)
                dve.wait_ge(ls_done, m + 1)
                dve.wait_ge(decay_made, m + 1)
                dve.scalar_tensor_tensor(out=s_lstm[:, b, :], in0=ps[:, 2 + b, 0:384], scalar=P ** -0.5,
                                         in1=decay[:, b, :], op0=ALU.mult, op1=ALU.mult).then_inc(ls_made, 1)
                dve.wait_ge(abs_made, m + 1)
                dve.wait_ge(emt_made, m + 1)
                own(dve.tensor_tensor(l_abs[:, b, :], l_abs[:, b, :], l_emt[:, b, :], ALU.max))
                own(dve.reciprocal(l_abs[:, b, :], l_abs[:, b, :]))
                dve.tensor_tensor(mix[:, 4 + m, :], ps[:, 4 + b, 0:T], l_abs[:, b, :], ALU.mult).then_inc(num_made, 1)
            for m in range(NM):
                if m % 2 == 0:
                    dve.wait_ge(lroot_made, m // 2 + 1)
                    own(dve.reciprocal(mix[:, m:m + 2, :], mix[:, m:m + 2, :]))
                x = mix[:, 4 + m, :]
                own(dve.scalar_tensor_tensor(out=x, in0=x, scalar=par_col("mlstm_norm_g_2", m), in1=mix[:, m, :],
                                             op0=ALU.mult, op1=ALU.mult))
                dve.tensor_tensor(x, x, og_s[:, m, :], ALU.mult).then_inc(mix_made, 1)
                dve.wait_ge(opa_hi_made, 8 * A_FILL["mix"] + 5 + m)
                dve.tensor_tensor(opa_lo[:, 4 + m, :], x, opa_hi[:, 4 + m, :].bitcast(F32),
                                  ALU.subtract).then_inc(opa_made, 1)
            for s in range(4):
                dve.wait_ge(g_done, MO + s + 1)
                for a in range(2):
                    k = 2 * s + a
                    ins = dve.scalar_tensor_tensor(out=xres[:, k, :], in0=pair(gbank(MO + s))[:, a, :],
                                                   scalar=mod_col(16 + k), in1=xres[:, k, :],
                                                   op0=ALU.mult, op1=ALU.add)
                evac(ins, MO + s)
                split_g(MO + s + 2)
        if last_stage >= 7:
            ffn(2, 6, "n6", lambda k: gmod[:, 8 + k:9 + k], 24)

        res = token_view(ybuf)
        for q in range(4):
            a, h = q % 2, q // 2
            dve.wait_ge(out_turned, q + 1)
            dve.tensor_copy(res[:, a, h * 512:(h + 1) * 512], ps[:, 4 + q, :]).then_inc(out_made, 1)

    @block.tensor
    def _(pe):
        def g_step(g, hi, lo, ready, tokens_out=False, slots=None, bank=None, waited=False):
            slot = g % 2
            b = gbank(g)
            if not waited:
                pe.wait_ge(g_hi_made, g + 1)
                pe.wait_ge(g_lo_made, g + 1)
                if g >= 4:
                    g_free(g - 4)
            for k in range(KT):
                ready(k)
                for a in range(2):
                    for n, (w, x) in enumerate(((g_hi, hi), (g_hi, lo), (g_lo, hi))):
                        wt, xt = w[:, slot, k, :], x[:, k, :]
                        st = dict(start=(k == 0 and a == 0 and n == 0), stop=(k == KT - 1 and n == 2),
                                  skip_group_check=True)
                        if tokens_out:
                            mm = pe.matmul(pair(b)[:, a, :], xt[:, a * P:(a + 1) * P], wt, **st)
                        else:
                            mm = pe.matmul(pair(b)[:, a, :], wt[:, a * P:(a + 1) * P], xt, **st)
            mm.then_inc(g_done, 1)

        def g_free(g):
            for f, first in enumerate(FFNS):
                if first <= g < first + FT:
                    pe.wait_ge(hid_made, FT * f + g - first + 1)
                    return
            pe.wait_ge(g_evac, evacs(g))

        def no_wait(k):
            pass

        def filled(signal, before, per=1):
            return lambda k: pe.wait_ge(signal, before + k // per + 1)

        def a_filled(fill):
            return filled(opa_made, 8 * A_FILL[fill])

        def sum_squares(n):
            for k in range(KT):
                if k % 2 == 0:
                    pe.wait_ge(sq_made, 4 * n + k // 2 + 1)
                mm = pe.matmul(ps[:, 0, 0:T], ones[:, :], ybuf[:, k, :], start=(k == 0), stop=(k == KT - 1))
            mm.then_inc(ss_done, 1)

        def ffn(f, norm, fill):
            g0, d0 = FFNS[f], FT * f
            sum_squares(norm)
            if f == 1:
                pe.wait_ge(ada_added, 6 * KT)
                for c in range(48):
                    mm = pe.matmul(ps[:, 1, c:c + 1], ada_acc[:, c * P:(c + 1) * P], ones[:, 0:1], start=True, stop=True)
                mm.then_inc(ada_summed, 1)
            g_step(g0, opa_hi, opa_lo, a_filled(fill))

            def d_step(i, r, s):
                if f == 1 and s == 0:
                    pe.wait_ge(mod_made, 2)
                pe.wait_ge(d_hi_made, i * 4 + (d0 + r + 1))
                pe.wait_ge(d_lo_made, i * 4 + (d0 + r + 1))
                pe.wait_ge(hid_lo_made, i * 4 + (d0 + r + 1))
                for a in range(KT):
                    for n, (w, x) in enumerate(((d_hi, hid_hi), (d_hi, hid_lo), (d_lo, hid_hi))):
                        mm = pe.matmul(pair(a // 2)[:, a % 2, :], w[:, r % 2, a * P:(a + 1) * P], x[:, r % 2, :],
                                       start=(s == 0 and a % 2 == 0 and n == 0), stop=(s == FT - 1 and n == 2),
                                       skip_group_check=True)
                mm.then_inc(d_done, 1)

            def both(i, r, s):
                pe.wait_ge(g_hi_made, i * 4 + (g0 + r + 2))
                pe.wait_ge(g_lo_made, i * 4 + (g0 + r + 2))
                if s is None or s >= 3:
                    pe.wait_ge(hid_made, i * 4 + (d0 + r - 2))
                else:
                    g_free(g0 + s + 1 - 4)
                g_step(g0 + r + 1, opa_hi, opa_lo, no_wait, waited=True)
                d_step(i, r, s)

            for r in range(4):
                both(0, r, r)
            with pe.Fori(1, 5) as i:
                for r in range(4):
                    both(i, r, None)
            both(5, 0, 20)
            d_step(5, 1, 21)

        pe.wait_ge(consts, c_basic)
        pe.wait_ge(x_loaded, 16)
        x_tok = token_view(ybuf)
        for k in range(KT):
            for a in range(TT):
                mm = pe.transpose(pair(k // 2)[:, k % 2, a * P:(a + 1) * P], x_tok[:, a, k * P:(k + 1) * P], ident[:, :])
            if k % 2 == 1:
                mm.then_inc(x_turned, 1)
        pe.wait_ge(par_loaded, 16 * N_PARAM_DMAS)
        pe.transpose(ps[:, 4, 0:P], prow[:, 0, :], ident[:, :])
        pe.transpose(ps[:, 4, P:NROWS], prow[0:NROWS - P, 1, :], ident[0:NROWS - P, 0:NROWS - P]).then_inc(par_turned, 1)

        sum_squares(0)
        for s in range(8):
            g_step(CV + s, opa_hi, opa_lo, a_filled("n0"))
        for s in range(4):
            g_step(BG + s, opa_hi, opa_lo, no_wait)
        for s in range(4):
            g_step(AO + s, opb_hi, opb_lo, filled(opb_made, 0, 2))
        if last_stage >= 2:
            ffn(0, 1, "n1")

        if last_stage >= 3:
            sum_squares(2)
            for s in range(6):
                g_step(KV + s, opa_hi, opa_lo, a_filled("n2") if s == 0 else no_wait, tokens_out=s in (3, 5))
            for w in range(2):
                c = CHUNKS.index(("cmp", w))
                pe.wait_ge(b_cmp_made, 2 * w + 2)
                pe.wait_ge(g_loaded[c % 2], 32 * (c // 2 + 1))
                for a in range(2):
                    for l in range(16):
                        mm = pe.matmul(ps[:, w, a * 64:(a + 1) * 64], w1_view(c % 2)[:, l, a * P:(a + 1) * P],
                                       b_cmp[:, l, :, :].rearrange("p g n -> p (g n)"), start=(l == 0), stop=(l == 15))
                mm.then_inc(cmp_hid_done, 1)
            for s in range(4):
                g_step(QG + s, opb_hi, opb_lo, filled(opb_made, 4) if s == 0 else no_wait)
            pe.wait_ge(side_lo, 2)
            for a in range(TT):
                for k in range(KT):
                    for n, (x, w) in enumerate(((opb_hi, qg_hi), (opb_lo, qg_hi), (opb_hi, qg_lo))):
                        mm = pe.matmul(ps[:, 3, 256 + 48 * a:304 + 48 * a], x[:, k, a * P:(a + 1) * P], w[:, k, :],
                                       start=(k == 0 and n == 0), stop=(k == KT - 1 and n == 2))
            mm.then_inc(gate_done, 1)
            pe.wait_ge(cmp_hid_silu, 3)
            pe.wait_ge(w2_loaded, 48)
            for a in range(2):
                pe.matmul(ps[:, 2, 0:64], w2_k[:, a, :, :].rearrange("p w n -> p (w n)"),
                          hid_cmp[:, 0, a, :, :].rearrange("p g n -> p (g n)"), start=(a == 0), stop=(a == 1))
            for a in range(2):
                mm = pe.matmul(ps[:, 2, 64:128], vrep[:, a, 0:P], w2_v[:, a, :], start=(a == 0), stop=(a == 1))
            mm.then_inc(kc_done, 1)
            pe.wait_ge(kc_made, 1)
            pe.wait_ge(g_evac, evacs(QG + 3))
            for a in range(TT):
                for h in range(NH):
                    lo = HD * (h % 2)
                    at = (a * 8 + h // 2) * 16
                    mm = pe.matmul(ps[:, h % 2, at:at + 16],
                                   q_t[lo:lo + HD, h // 2, a * P:(a + 1) * P], kc_dup[lo:lo + HD, h // 4, :],
                                   start=True, stop=True)
            mm.then_inc(cs_done, 1)
            pe.wait_ge(cs_made, 1)
            for q in range(2):
                for a in range(TT):
                    mm = pe.transpose(ps[:, 7, (2 * q + a) * P:(2 * q + a + 1) * P],
                                      ctmp[:, q * T + a * P:q * T + (a + 1) * P], ident[:, :])
            mm.then_inc(pct_done, 1)

            def scores(h):
                if h >= 2:
                    pe.wait_ge(shifted, h - 1)
                lo, g = HD * (h % 2), h // 4
                for a, w in ((1, 256), (0, 128)):
                    for b in range(2):
                        mm = pe.matmul(ps[:, 2 * (h % 2) + (1 - a), b * w:(b + 1) * w],
                                       q_t[lo:lo + HD, h // 2, a * P:(a + 1) * P], k_dup[lo:lo + HD, b, g, 0:w],
                                       start=True, stop=True)
                mm.then_inc(scored, 1)

            pe.wait_ge(kc_made, 2)
            scores(0)
            scores(1)
            for h in range(NH):
                pe.wait_ge(scaled, h + 1)
                if h >= 1:
                    pe.wait_ge(pt_slc, h)
                    pe.wait_ge(pt_win, h)
                e = e_buf[:, h % 3, :]
                for b in range(2):
                    for lo, at in ((512 + b * P, 0), (b * 256, P), (b * 256 + P, 2 * P)):
                        mm = pe.transpose(ps[:, 4 + b, at:at + P], e[:, lo:lo + P], ident[:, :])
                mm.then_inc(pt_done, 1)
                if h + 2 < NH:
                    scores(h + 2)
                pe.wait_ge(pt_slc, h + 1)
                pe.wait_ge(pt_win, h + 1)
                pe.wait_ge(pct_made, 1)
                j, lo, v = h // 2, HD * (h % 2), HD * (h // 4)
                if j >= 2:
                    pe.wait_ge(opa_made, 8 * A_FILL["attn"] + j - 1)
                o = ps[lo:lo + HD, 6 + j % 2, 0:T]
                n = 0
                for b in range(2):
                    for s, ob, pb in ((0, o, pt_buf[:, b, 0:256]), (1, o[:, P:T], pt_buf[:, b, 256:384])):
                        pe.matmul(ob, v_tok[:, b, s, v:v + HD], pb, start=(n == 0), stop=False, skip_group_check=True)
                        n += 1
                pe.matmul(o, vc_blk[:, h // 2, :], pct[:, h % 2, :], start=False, stop=True,
                          skip_group_check=True).then_inc(pv_done, 1)
            for s in range(4):
                g_step(WO + s, opa_hi, opa_lo, a_filled("attn") if s == 0 else no_wait)
        if last_stage >= 4:
            ffn(1, 3, "n3")

        if last_stage >= 5:
            sum_squares(4)
            pe.wait_ge(consts, c_comb)
            for a, lo, w in ((1, 0, 256), (0, 256, 128)):
                for i, r in ((0, 4), (1, 16)):
                    mm = pe.matmul(ps[:, 1, lo:lo + w], comb[0:r, i, a * P:(a + 1) * P], comb[0:r, i, 0:w],
                                   start=(i == 0), stop=(i == 1))
            mm.then_inc(comb_done, 1)
            sum_squares(5)
            for s in range(14):
                g = MX + s
                g_step(g, opa_hi, opa_lo, a_filled("n5") if s == 0 else no_wait,
                       tokens_out=MX_VA <= g < MX_QM or MX_VM <= g < MX_OG)

        if last_stage >= 6:
            g_free(MX_OG + 1)
            for a in range(TT):
                for k in range(KT):
                    for n, (x, w) in enumerate(((opa_hi, if_hi), (opa_lo, if_hi), (opa_hi, if_lo))):
                        mm = pe.matmul(ps[:, 4, 8 * a:8 * a + 8], x[:, k, a * P:(a + 1) * P], w[:, k, :],
                                       start=(k == 0 and n == 0), stop=(k == KT - 1 and n == 2))
            mm.then_inc(if_done, 1)
            for k in range(KT):
                if k % 2 == 0:
                    pe.wait_ge(qk_sq, k // 2 + 1)
                mm = pe.matmul(pair(k // 2)[:, k % 2, :], ones64[:, :], ybuf[:, k, :], start=True, stop=True)
                if k % 2 == 1:
                    mm.then_inc(qk_ss, 1)
            pe.wait_ge(if_tok_made, 1)
            for i in range(2):
                for a in range(TT):
                    mm = pe.transpose(ps[0:NM, 5, i * T + a * P:i * T + (a + 1) * P], if_tok[:, a, 4 * i:4 * i + 4],
                                      ident[:, :])
            mm.then_inc(rows_turned, 1)
            pe.wait_ge(rows_made, 1)
            for a in range(TT):
                mm = pe.transpose(ps[:, 4, 16 + 4 * a:20 + 4 * a], rows[:, 3, a * P:(a + 1) * P], ident[0:NM, 0:NM])
            mm.then_inc(a_turned, 1)
            pe.wait_ge(qk_made, 4)
            pe.wait_ge(a_made, 1)

            def dil_scores(h):
                if h >= 2:
                    pe.wait_ge(shifted, NH + h - 1)
                lo, j = HD * (h % 2), h // 2
                for a, at, w in ((1, 0, 256), (0, 256, 128)):
                    mm = pe.matmul(ps[:, h % 2, at:at + w], qk_a[lo:lo + HD, j, a * P:(a + 1) * P],
                                   qk_a[lo:lo + HD, 4 + j, 0:w], start=True, stop=True)
                mm.then_inc(scored, 1)

            dil_scores(0)
            dil_scores(1)
            for h in range(NH2):
                pe.wait_ge(scaled, NH + h + 1)
                if h >= 2:
                    pe.wait_ge(pt_slc, NH + h - 1)
                e = e_dil[:, h % 3, :]
                for lo, at in ((256, 0), (0, P), (P, 2 * P)):
                    mm = pe.transpose(ps[:, 4 + h % 2, at:at + P], e[:, lo:lo + P], ident[:, :])
                mm.then_inc(pt_done, 1)
                if h + 2 < NH2:
                    dil_scores(h + 2)
                pe.wait_ge(pt_slc, NH + h + 1)
                j, lo = h // 2, HD * (h % 2)
                if j >= 2:
                    pe.wait_ge(opa_made, 8 * A_FILL["mix"] + j - 1)
                o = ps[lo:lo + HD, 6 + j % 2, 0:T]
                pe.matmul(o, v_a[:, 0, h * HD:(h + 1) * HD], pt_dil[:, h % 2, 0:256], start=True, stop=False,
                          skip_group_check=True)
                pe.matmul(o[:, P:T], v_a[:, 1, h * HD:(h + 1) * HD], pt_dil[:, h % 2, 256:384], start=False, stop=True,
                          skip_group_check=True).then_inc(pv_done, 1)
            pe.wait_ge(shifted, NH + NH2)
            pe.wait_ge(pt_slc, NH + NH2)
            pe.wait_ge(conv_ready_made, 4)
            pe.wait_ge(opa_made, 8 * A_FILL["mix"] + 4)

            def lstm_scores(m):
                b = m % 2
                if m >= 2:
                    pe.wait_ge(num_made, m - 1)
                for i in range(2):
                    mm = pe.matmul(ps[:, b, i * T:(i + 1) * T], sel4[:, m, :], rows[:, 5 + i, :], start=True, stop=True)
                mm.then_inc(m_cast, 1)
                q, k = qk_m[:, m, :], qk_m[:, 4 + m, :]
                pe.matmul(ps[:, 2 + b, 0:256], k[:, 0:P], q, start=True, stop=True)
                pe.matmul(ps[:, 2 + b, 256:384], k[:, P:T], q[:, P:T], start=True, stop=True).then_inc(ls_done, 1)

            lstm_scores(0)
            lstm_scores(1)
            for m in range(NM):
                b = m % 2
                pe.wait_ge(ls_made, m + 1)
                for i in range(2):
                    for s in range(2):
                        w = v_m[:, s, m * P:(m + 1) * P] if i == 0 else ones[:, :]
                        o = ps[:, 4 + b, i * T + s * P:(i + 1) * T]
                        x = s_lstm[:, b, 256 * s:256 + 128 * s]
                        mm = pe.matmul(o, w, x, start=(s == 0), stop=(s == 1), skip_group_check=True)
                mm.then_inc(num_done, 1)
                if m + 2 < NM:
                    lstm_scores(m + 2)
                pe.wait_ge(lsq_made, m + 1)
                pe.matmul(pair(6 + m // 2)[:, b, :], ones[:, :], l_sq[:, b, :], start=True, stop=True).then_inc(lss_done, 1)
            for s in range(4):
                g_step(MO + s, opa_hi, opa_lo, a_filled("mix") if s == 0 else no_wait, waited=False)
        if last_stage >= 7:
            ffn(2, 6, "n6")

        for q in range(4):
            pe_ready = {1: 1, 2: 2, 3: 3, 4: 4, 5: 5, 6: 6, 7: 7}[last_stage]
            piece_ready(pe, pe_ready, 2 * (q // 2) + 1)
            a = q % 2
            for k in range(4 * (q // 2), 4 * (q // 2) + 4):
                mm = pe.transpose(ps[:, 4 + q, (k % 4) * P:(k % 4 + 1) * P], xres[:, k, a * P:(a + 1) * P], ident[:, :])
            mm.then_inc(out_turned, 1)
    return ctx


_OUT = (1, T, D)


def kernel(**inputs):
    import numpy as np
    import concourse.bacc as bacc
    from concourse.bass_utils import run_bass_kernel_spmd

    nc = bacc.Bacc("TRN2", target_bir_lowering=False, num_devices=1)
    arrays, t = {}, {}
    for name, value in inputs.items():
        a = np.ascontiguousarray(value)
        arrays["in_" + name] = a
        t[name] = nc.dram_tensor("in_" + name, a.shape, mybir.dt.from_np(a.dtype), kind="ExternalInput").ap()
    out = nc.dram_tensor("out_x", _OUT, F32, kind="ExternalOutput").ap()
    with layer_kernel(nc, t, out):
        pass
    r = run_bass_kernel_spmd(nc, [arrays], core_ids=[0])
    return r.results[0]["out_x"]
```

```python
from contextlib import ExitStack

import concourse.bass as bass
from concourse import mybir

F32 = mybir.dt.float32
F32R = mybir.dt.float32r
ALU = mybir.AluOpType
ACT = mybir.ActivationFunctionType
AX_X = mybir.AxisListType.X

P = 128
T = 256
TT = T // P
D = 1024
KT = D // P
FFN = 2816
FT = FFN // P
NH, NG = 16, 4
HD = 64
NH2 = 8
NM = 4
NEG = -1e30
SLOPES = [2.0 ** (-8.0 * (h + 1) / NH) for h in range(NH)]

ROWS, NROWS = {}, 0
for _name, _n in (("a_norm", 8), ("kv_norm", 8), ("b_norm", 8), ("f_norm", 16), ("final_norm", 8),
                  ("g_mix_2", 8), ("g_ffn_2", 8), ("c_2", 8), ("a_conv", 24), ("w_conv_2", 32),
                  ("b_conv_2", 8), ("b_ada_2", 48), ("mlstm_norm_g_2", 4), ("cmp_pe_k", 16),
                  ("cmp_pe_v", 16)):
    ROWS[_name] = NROWS
    NROWS += _n
ROWS["q_norm_g_2"], ROWS["k_norm_g_2"] = NROWS, NROWS + 1
NROWS += 2
N_PARAM_DMAS = 15 + 4

CV, BG, AO = 0, 8, 12
F0 = 16
KV = F0 + FT
QG = KV + 6
WO = QG + 4
F1 = WO + 4
MX = F1 + FT
MO = MX + 14
F2 = MO + 4
GTOTAL = F2 + FT
FFNS = (F0, F1, F2)
MX_QA, MX_KA, MX_VA, MX_QM, MX_KM, MX_VM, MX_OG = (MX + 2 * n for n in range(7))


def plan_chunks():
    chunks, chunk_of = [], {}

    def steps(first, n, pair):
        for g in range(first, first + n, 2):
            chunk_of[g] = chunk_of[g + 1] = len(chunks)
            chunks.append(("pair" if pair else "flat", g))

    steps(CV, 8, True)
    steps(BG, 4, False)
    steps(AO, 4, False)
    steps(F0, FT, True)
    steps(KV, 6, False)
    steps(QG, 4, False)
    chunks.append(("cmp", 0))
    chunks.append(("cmp", 1))
    steps(WO, 4, False)
    steps(F1, FT, True)
    steps(MX, 14, False)
    steps(MO, 4, False)
    steps(F2, FT, True)
    return chunks, chunk_of


CHUNKS, CHUNK_OF = plan_chunks()


def layer_kernel(nc, t, out, last_stage=7):
    ctx = ExitStack()

    def sb(name, shape, dt=F32, on=ctx):
        return on.enter_context(nc.sbuf_tensor(name, shape, dt))

    def sem(name):
        return ctx.enter_context(nc.semaphore(name))

    g_raw = sb("g_raw", [P, 2, KT, 512])
    g_hi = sb("g_hi", [P, 2, KT, 256], F32R)
    g_lo = sb("g_lo", [P, 2, KT, 256], F32R)
    xres = sb("xres", [P, KT, T])
    opa_hi = sb("opa_hi", [P, KT, T], F32R)
    opa_lo = sb("opa_lo", [P, KT, T], F32R)
    ybuf = sb("ybuf", [P, KT, T])
    gu = sb("gu", [P, 2, 2, T])
    hid_hi = sb("hid_hi", [P, 2, T], F32R)
    hid_lo = sb("hid_lo", [P, 2, T], F32R)
    rstd = sb("rstd", [P, T])
    ident = sb("ident", [P, P])
    ones = sb("ones", [P, P])
    ones64 = sb("ones64", [P, P])
    eps = sb("eps", [P, 2])
    par = sb("par", [P, NROWS])
    csil = sb("csil", [P, KT])
    mod = sb("mod", [P, 48])
    gmod = sb("gmod", [P, 16])
    zpad = sb("zpad", [P, 2, T + 4])
    qg_raw = sb("qg_raw", [P, KT, 48])
    qg_hi = sb("qg_hi", [P, KT, 48], F32R)
    qg_lo = sb("qg_lo", [P, KT, 48], F32R)
    if_raw = sb("if_raw", [P, KT, 8])
    if_hi = sb("if_hi", [P, KT, 8], F32R)
    if_lo = sb("if_lo", [P, KT, 8], F32R)
    if_bias = sb("if_bias", [NM, 2])
    gates = sb("gates", [P, TT, 48])
    nmax = sb("nmax", [P, 3, 4])
    zsum = sb("zsum", [P, 3, 4])
    fac = sb("fac", [P, 3, 4])
    dist = sb("dist", [P, 384])
    cmp_bias = sb("cmp_bias", [P, TT, NH, 16])
    any_vis = sb("any_vis", [P, TT])
    dil_count = sb("dil_count", [P, 384])
    dil_mask = sb("dil_mask", [P, 384])
    lstm_mask = sb("lstm_mask", [P, 384])
    sel4 = sb("sel4", [NM, NM, P])
    small = sb("small", [P, 64])
    cfac = sb("cfac", [P, TT, NH])

    over = ExitStack()
    ada_acc = sb("ada_acc", [P, 6 * D], on=over)
    ada_raw = sb("ada_raw", [P, 2, D], on=over)
    over.close()
    over = ExitStack()
    qk_a = sb("qk_a", [P, KT, T], on=over)
    v_a = sb("v_a", [P, TT, 512], on=over)
    qk_m = sb("qk_m", [P, KT, T], on=over)
    v_m = sb("v_m", [P, TT, 512], on=over)
    og_s = sb("og_s", [P, NM, T], on=over)
    a_col = sb("a_col", [P, TT, NM], on=over)
    comb = sb("comb", [16, 2, T], on=over)
    sb("pad_a", [P, 8192 - 7168 - 8 - 512], on=over)
    ctx.push(over)

    over_b = ExitStack()
    opb_hi = sb("opb_hi", [P, KT, T], F32R, on=over_b)
    opb_lo = sb("opb_lo", [P, KT, T], F32R, on=over_b)
    d_raw = sb("d_raw", [P, 2, 2, D], on=over_b)
    d_hi = sb("d_hi", [P, 2, D], F32R, on=over_b)
    d_lo = sb("d_lo", [P, 2, D], F32R, on=over_b)
    over_b.close()
    over_b = ExitStack()
    e_buf = sb("e_buf", [P, 3, 768], on=over_b)
    pt_buf = sb("pt_buf", [P, 2, 384], on=over_b)
    bias_h = sb("bias_h", [P, 2, 384], on=over_b)
    sb("pad_b", [P, 4096 - 3840], on=over_b)
    k_dup = sb("k_dup", [P, 2, NG, T], on=over_b)
    v_tok = sb("v_tok", [P, 2, TT, T], on=over_b)
    x_cmp = sb("x_cmp", [P, 2, NG, 288], on=over_b)
    b_cmp = sb("b_cmp", [P, 16, NG, 16], on=over_b)
    vc_blk = sb("vc_blk", [P, NH, HD], on=over_b)
    hid_cmp = sb("hid_cmp", [P, 2, 2, NG, 16], on=over_b)
    kc_blk = sb("kc_blk", [P, NG, 2, 16], on=over_b)
    w2_k = sb("w2_k", [P, 2, 2, HD], on=over_b)
    w2_v = sb("w2_v", [P, 2, HD], on=over_b)
    over_b.close()
    over_b = ExitStack()
    e_dil = sb("e_dil", [P, 3, 384], on=over_b)
    pt_dil = sb("pt_dil", [P, 2, 384], on=over_b)
    rows = sb("rows", [NM, 7, T], on=over_b)
    ones_row = sb("ones_row", [NM, T], on=over_b)
    decay = sb("decay", [P, NM, 384], on=over_b)
    l_abs = sb("l_abs", [P, NM, T], on=over_b)
    l_emt = sb("l_emt", [P, NM, T], on=over_b)
    l_sq = sb("l_sq", [P, NM, T], on=over_b)
    mix = sb("mix", [P, KT, T], on=over_b)
    over_b.close()
    over_b = ExitStack()
    prow = sb("prow", [P, 2, P], on=over_b)
    over_b.close()
    sb("over_b_extent", [P, 12288])

    ps = ctx.enter_context(nc.psum_tensor("ps", [P, 8, 512], F32))

    x_loaded, par_loaded, side_loaded = sem("x_loaded"), sem("par_loaded"), sem("side_loaded")
    g_loaded = [sem("g_loaded0"), sem("g_loaded1")]
    d_loaded = [sem("d_loaded0"), sem("d_loaded1")]
    ada_loaded = [sem("ada_loaded0"), sem("ada_loaded1")]
    w2_loaded, pad_made, kc_zeroed = sem("w2_loaded"), sem("pad_made"), sem("kc_zeroed")
    stored = sem("stored")
    consts = sem("consts")
    g_hi_made, g_lo_made = sem("g_hi_made"), sem("g_lo_made")
    d_hi_made, d_lo_made = sem("d_hi_made"), sem("d_lo_made")
    side_hi, side_lo = sem("side_hi"), sem("side_lo")
    g_done, g_evac = sem("g_done"), sem("g_evac")
    d_done = sem("d_done")
    opa_hi_made, opa_made = sem("opa_hi_made"), sem("opa_made")
    opb_hi_made, opb_made = sem("opb_hi_made"), sem("opb_made")
    x_turned, xres_made = sem("x_turned"), sem("xres_made")
    par_turned, par_made = sem("par_turned"), sem("par_made")
    csil_made = sem("csil_made")
    ada_scaled, ada_added, ada_summed, mod_made = sem("ada_scaled"), sem("ada_added"), sem("ada_summed"), sem("mod_made")
    res_added = sem("res_added")
    sq_made, ss_done, rms_made = sem("sq_made"), sem("ss_done"), sem("rms_made")
    y_made = sem("y_made")
    sq_added, sqg_made, ms_made = sem("sq_added"), sem("sqg_made"), sem("ms_made")
    c_copied = sem("c_copied")
    gu_made, gate_scaled, k_copied, r_turned = sem("gu_made"), sem("gate_scaled"), sem("k_copied"), sem("r_turned")
    silu_made, hid_made, hid_hi_made, hid_lo_made = (sem("silu_made"), sem("hid_made"),
                                                     sem("hid_hi_made"), sem("hid_lo_made"))
    kv_copied = sem("kv_copied")
    b_cmp_made, cmp_hid_done, cmp_hid_silu = sem("b_cmp_made"), sem("cmp_hid_done"), sem("cmp_hid_silu")
    kc_done, kc_made = sem("kc_done"), sem("kc_made")
    gate_done, gate_exp, gate_turned, gates_made = (sem("gate_done"), sem("gate_exp"), sem("gate_turned"),
                                                    sem("gates_made"))
    cs_done, cs_shift, cs_exp, cs_made = sem("cs_done"), sem("cs_shift"), sem("cs_exp"), sem("cs_made")
    pct_done, pct_made = sem("pct_done"), sem("pct_made")
    bias_made = sem("bias_made")
    scored, shifted, exp_made, scaled = sem("scored"), sem("shifted"), sem("exp_made"), sem("scaled")
    pt_done, pt_slc, pt_win, pv_done = sem("pt_done"), sem("pt_slc"), sem("pt_win"), sem("pv_done")
    comb_done = sem("comb_done")
    z_copied, conv_made = sem("z_copied"), sem("conv_made")
    qk_sq, qk_ss, qk_root, qk_made = sem("qk_sq"), sem("qk_ss"), sem("qk_root"), sem("qk_made")
    og_made = sem("og_made")
    if_done, if_in, if_abs = sem("if_done"), sem("if_in"), sem("if_abs")
    rows_made, a_turned, a_made = sem("rows_made"), sem("a_turned"), sem("a_made")
    m_cast, arg_made, decay_made, emt_made = (sem("m_cast"), sem("arg_made"), sem("decay_made"),
                                              sem("emt_made"))
    ls_done, ls_made, num_done, abs_made, num_made = (sem("ls_done"), sem("ls_made"), sem("num_done"),
                                                      sem("abs_made"), sem("num_made"))
    lsq_made, lss_done, lroot_made, mix_made = (sem("lsq_made"), sem("lss_done"), sem("lroot_made"),
                                                sem("mix_made"))
    out_turned, out_made = sem("out_turned"), sem("out_made")
    dve_own = sem("dve_own")

    conv_ready_made = sem("conv_ready_made")
    c_basic, c_block1 = 6, 6 + 21
    c_comb, c_dil = c_block1 + 3, c_block1 + 3 + 6

    def halves(ap):
        return ap.rearrange("p k (two n) -> p k two n", two=2)

    def pair(bank, n=T):
        return ps[:, bank, 0:2 * n].rearrange("p (a n) -> p a n", a=2)

    def evacs(g):
        return g + 1 - FT * sum(g >= f + FT for f in FFNS) - max(0, min(2, g + 1 - MX_OG))

    def gbank(g):
        return 4 + g % 4

    def token_view(tile):
        return tile[:, :, :].rearrange("p k t -> p (k t)").rearrange("p (a d) -> p a d", a=TT)

    def w1_view(slot):
        return g_raw[:, slot, :, :].rearrange("p k n -> p (k n)").rearrange("p (l n) -> p l n", l=16)

    def par_col(name, i=0, n=1):
        return par[:, ROWS[name] + i:ROWS[name] + i + n]

    def raw_step(g):
        c = CHUNK_OF[g]
        return raw_cols(c % 2, g % 2, CHUNKS[c][0] == "pair")

    def raw_cols(slot, half, paired):
        if paired:
            return halves(g_raw[:, slot, :, :])[:, :, :, half * P:(half + 1) * P]
        return g_raw[:, slot, :, half * 256:(half + 1) * 256]

    def part_view(parts, g, paired):
        return halves(parts[:, g % 2, :, :]) if paired else parts[:, g % 2, :, :]

    def mod_col(i):
        return mod[:, i:i + 1]

    q_t = ybuf
    r_next = gu[:, 0, 0, :]
    r_sq = gu[:, 0, 1, :]
    pct = gu[:, 0, :, :]
    gate_row = gu[0:48, 0, 0, :]
    vrep = gu[:, 1, :, :]
    r_col = small[:, 10:12]
    ctmp = e_buf[:, 2, 0:2 * T]
    blk16 = small[:, 0:8]
    cmax = small[:, 16:48]
    def kv_tiles(s):
        return gu[:, s % 4 // 2 if s >= 2 else s, :, :]

    q_gain = small[:, 8:9]

    def c4(ap):
        return ap.rearrange("p (x n) -> p x n", n=16)

    A_FILL = {"n0": 0, "n1": 1, "n2": 2, "attn": 3, "n5": 4, "mix": 5, "n6": 6}
    B_FILL = {"b": 4, "n3": 12}

    def piece_ready(eng, n, j):
        if n == 0:
            eng.wait_ge(xres_made, 4)
        elif n in (1, 3, 6):
            eng.wait_ge(g_evac, evacs({1: AO, 3: WO, 6: MO}[n] + j))
        else:
            eng.wait_ge(res_added, {2: 0, 4: 4, 5: 8, 7: 12}[n] + j + 1)

    Y_BASE = {5: 0, 6: 8}
    glimit = {1: F0, 2: KV, 3: F1, 4: MX, 5: MO, 6: F2, 7: GTOTAL}[last_stage]
    climit = CHUNK_OF[glimit - 1] + 1

    def released(eng, c):
        if c < 0:
            return
        kind, g = CHUNKS[c]
        if kind == "cmp":
            eng.wait_ge(cmp_hid_done, g + 1)
        else:
            eng.wait_ge(g_hi_made, g + 2)
            eng.wait_ge(g_lo_made, g + 2)

    def weight_of(g):
        if g < BG:
            j = (g - CV) // 2
            return t["a_w_in"][0], t["a_w_in"][0], D + 256 * j, 2 * D + 256 * j
        for first, n, w in ((BG, 4, t["a_w_in"][0]), (AO, 4, t["a_w_out"][0]), (KV, 6, t["w_kv"]),
                            (QG, 4, t["b_w_qg"][0]), (WO, 4, t["b_w_o"][0]),
                            (MX, 14, t["w_in_2"][0]), (MO, 4, t["w_out_2"][0])):
            if first <= g < first + n:
                return w, None, 256 * (g - first), None
        f = [F0 <= g < KV, F1 <= g < MX, F2 <= g].index(True)
        return (*ffn_weights(f), 128 * (g - FFNS[f]), None)

    def ffn_weights(f):
        if f == 2:
            return t["w_gate_2"][0], t["w_up_2"][0]
        return t["f_w_gu"][f][:, 0:FFN], t["f_w_gu"][f][:, FFN:2 * FFN]

    def down_weight(f):
        return t["w_down_2"][0] if f == 2 else t["f_w_down"][f]

    def by_tile(w):
        return w.rearrange("(k p) n -> p k n", p=P)

    def load_params(eng, part):
        loads = []
        for name, n in (("a_norm", 8), ("kv_norm", 8), ("b_norm", 8), ("f_norm", 16), ("final_norm", 8),
                        ("g_mix_2", 8), ("g_ffn_2", 8), ("c_2", 8), ("a_conv", 24), ("w_conv_2", 32),
                        ("b_conv_2", 8), ("b_ada_2", 48), ("mlstm_norm_g_2", 4)):
            src = t[name]
            if len(src.shape) == 3:
                src = src.rearrange("a j (k p) -> (a j k) p", p=P)
            elif len(src.shape) == 2:
                src = src.rearrange("a (k p) -> (a k) p", p=P)
            else:
                src = src.rearrange("(k p) -> k p", p=P)
            r0, half = ROWS[name] % P, ROWS[name] // P
            loads.append((prow[r0:r0 + n, half, :], src))
        for name in ("cmp_pe_k", "cmp_pe_v"):
            r0 = ROWS[name] - P
            loads.append((prow[r0:r0 + 16, 1, :], t[name].rearrange("(l two) d -> l (two d)", two=2)))
        for name in ("q_norm_g_2", "k_norm_g_2"):
            r0 = ROWS[name] - P
            for lo in (0, HD):
                loads.append((prow[r0:r0 + 1, 1, lo:lo + HD], t[name]))
        assert len(loads) == N_PARAM_DMAS
        for dst, src in loads[part::2]:
            eng.dma_start(dst, src).then_inc(par_loaded, 16)

    block = ctx.enter_context(nc.Block())

    @block.sync
    def _(sp):
        def load_pair(slot, wa, wb, ca, cb):
            v = halves(g_raw[:, slot, :, :])
            sp.dma_start(v[:, :, 0, :], by_tile(wa)[:, :, bass.ds(ca, 256)]).then_inc(g_loaded[slot], 16)
            sp.dma_start(v[:, :, 1, :], by_tile(wb)[:, :, bass.ds(cb, 256)]).then_inc(g_loaded[slot], 16)

        def load_g(c):
            slot = c % 2
            released(sp, c - 2)
            kind, g = CHUNKS[c]
            if kind == "cmp":
                w = t["cmp_w1_v" if g else "cmp_w1_k"].rearrange("(l p) n -> p l n", p=P)
                for l in (0, 8):
                    sp.dma_start(w1_view(slot)[:, l:l + 8, :], w[:, l:l + 8, :]).then_inc(g_loaded[slot], 16)
                return
            wa, wb, ca, cb = weight_of(g)
            if kind == "pair":
                load_pair(slot, wa, wb, ca, ca if cb is None else cb)
                return
            for k in (0, 4):
                sp.dma_start(g_raw[:, slot, k:k + 4, :],
                             by_tile(wa)[:, k:k + 4, ca:ca + 512]).then_inc(g_loaded[slot], 16)

        def load_d(f, c, slot):
            src = down_weight(f).rearrange("(c j p) n -> p c j n", j=2, p=P)
            sp.dma_start(d_raw[:, slot:slot + 1, :, :], src[:, bass.ds(c, 1), :, :]).then_inc(d_loaded[slot], 16)

        def load_ffn(f):
            c0, g0, d0, dc0 = CHUNK_OF[FFNS[f]], FFNS[f], FT * f, FT // 2 * f
            for c in range(3):
                load_g(c0 + c)
                if c == 0 and f > 0:
                    sp.wait_ge(g_done, (WO if f == 1 else MO) + 1)
                if dc0 + c >= 2:
                    sp.wait_ge(d_hi_made, 2 * (dc0 + c - 1))
                    sp.wait_ge(d_lo_made, 2 * (dc0 + c - 1))
                load_d(f, c, (dc0 + c) % 2)
            wa, wb = ffn_weights(f)
            with sp.Fori(0, 4) as i:
                for r in range(2):
                    sp.wait_ge(g_hi_made, i * 4 + (g0 + 4 + 2 * r))
                    sp.wait_ge(g_lo_made, i * 4 + (g0 + 4 + 2 * r))
                    load_pair((c0 + 3 + r) % 2, wa, wb, i * 512 + 256 * (3 + r), i * 512 + 256 * (3 + r))
                    sp.wait_ge(d_hi_made, i * 4 + (d0 + 4 + 2 * r))
                    sp.wait_ge(d_lo_made, i * 4 + (d0 + 4 + 2 * r))
                    load_d(f, i * 2 + (3 + r), (dc0 + 3 + r) % 2)

        c = 0
        while c < climit:
            g = CHUNKS[c][1] if CHUNKS[c][0] != "cmp" else -1
            if g in FFNS:
                load_ffn(FFNS.index(g))
                c += FT // 2
            else:
                load_g(c)
                c += 1
                if c == 1:
                    load_params(sp, 1)
                if g == KV + 4:
                    sp.wait_ge(d_done, FT)
                    for w in range(2):
                        sp.dma_start(w2_k[:, :, w, :], t["cmp_w2_k"].rearrange("(a p) n -> p a n", p=P)).then_inc(w2_loaded, 16)
                    sp.dma_start(w2_v[:, :, :], t["cmp_w2_v"].rearrange("(a p) n -> p a n", p=P)).then_inc(w2_loaded, 16)
        res = token_view(ybuf)
        dst = out[0].rearrange("(a p) d -> p a d", p=P)
        for q in range(4):
            a, h = q % 2, q // 2
            sp.wait_ge(out_made, q + 1)
            sp.dma_start(dst[:, a, h * 512:(h + 1) * 512], res[:, a, h * 512:(h + 1) * 512]).then_inc(stored, 16)
        sp.wait_ge(stored, 64)

    @block.gpsimd
    def _(pool):
        made = [0]

        def const(ins):
            made[0] += 1
            ins.then_inc(consts, 1)
            pool.wait_ge(consts, made[0])

        const(pool.memset(ident[:, :], 0.0))
        const(pool.affine_select(out=ident[:, :], in_=ident[:, :], compare_op=ALU.not_equal, fill=1.0,
                                 base=0, pattern=[[-1, P]], channel_multiplier=1))
        const(pool.memset(ones[:, :], 1.0))
        const(pool.memset(eps[:, 0:1], 1e-5))
        const(pool.memset(eps[:, 1:2], 1e-6))
        const(pool.memset(zpad[:, :, 0:4], 0.0))
        assert made[0] == c_basic

        w_ada = t["w_ada_2"][0].rearrange("(k p) n -> p k n", p=P)

        def load_ada(m):
            n, k = m // KT, m % KT
            pool.dma_start(ada_raw[:, m % 2, :], w_ada[:, k, n * D:(n + 1) * D]).then_inc(ada_loaded[m % 2], 16)

        const(pool.memset(ones64[:, :], 0.0))
        const(pool.memset(ones64[0:HD, 0:HD], 1.0))
        const(pool.memset(ones64[HD:P, HD:P], 1.0))
        for a, lo, w in ((1, 0, 256), (0, 256, 128)):
            d = dist[:, lo:lo + w]
            const(pool.iota(d, pattern=[[1, w]], base=-P * a, channel_multiplier=-1,
                            allow_small_or_imprecise_dtypes=True))
            const(pool.affine_select(out=d, in_=d, compare_op=ALU.is_ge, fill=NEG, base=P * a,
                                     pattern=[[-1, w]], channel_multiplier=1))
        cd = cmp_bias[:, :, 0, :]
        const(pool.iota(cd, pattern=[[-P, TT], [16, 16]], base=0, channel_multiplier=-1,
                        allow_small_or_imprecise_dtypes=True))
        const(pool.tensor_scalar(cd, cd, 15.5, None, ALU.add))
        const(pool.affine_select(out=cd, in_=cd, compare_op=ALU.is_ge, fill=NEG, base=-31,
                                 pattern=[[P, TT], [-16, 16]], channel_multiplier=1))
        for h in range(NH - 1, -1, -1):
            last = pool.tensor_scalar(cmp_bias[:, :, h, :], cd, SLOPES[h], None, ALU.mult)
        const(last)
        const(pool.memset(any_vis[:, :], 1.0))
        const(pool.affine_select(out=any_vis[:, 0:1], in_=any_vis[:, 0:1], compare_op=ALU.is_ge, fill=0.0,
                                 base=-31, pattern=[[0, 1]], channel_multiplier=1))
        const(pool.memset(blk16, 1.0))
        const(pool.affine_select(out=blk16, in_=blk16, compare_op=ALU.is_ge, fill=0.0, base=0,
                                 pattern=[[-16, 8]], channel_multiplier=1))
        const(pool.affine_select(out=blk16, in_=blk16, compare_op=ALU.is_ge, fill=0.0, base=15,
                                 pattern=[[16, 8]], channel_multiplier=-1))
        const(pool.memset(lstm_mask[:, :], 0.0))
        for lo, w in ((0, 256), (256, 128)):
            m = lstm_mask[:, lo:lo + w]
            const(pool.affine_select(out=m, in_=m, compare_op=ALU.is_ge, fill=NEG, base=0,
                                     pattern=[[1, w]], channel_multiplier=-1))
        const(pool.memset(sel4[:, :, :], 0.0))
        const(pool.affine_select(out=sel4[:, :, :], in_=sel4[:, :, :], compare_op=ALU.not_equal, fill=1.0,
                                 base=0, pattern=[[-1, NM], [0, P]], channel_multiplier=1))
        assert made[0] == c_block1

        pool.wait_ge(csil_made, 1)
        load_ada(0)
        load_ada(1)
        for m in range(6 * KT):
            n, k = m // KT, m % KT
            acc = ada_acc[:, n * D:(n + 1) * D]
            pool.wait_ge(ada_loaded[m % 2], 16 * (m // 2 + 1))
            if k == 0:
                ins = pool.tensor_scalar(acc, ada_raw[:, m % 2, :], csil[:, k:k + 1], None, ALU.mult)
            else:
                raw = ada_raw[:, m % 2, :]
                pool.tensor_scalar(raw, raw, csil[:, k:k + 1], None, ALU.mult).then_inc(ada_scaled, 1)
                pool.wait_ge(ada_scaled, m - n)
                ins = pool.tensor_tensor(acc, acc, raw, ALU.add)
            ins.then_inc(ada_added, 1)
            pool.wait_ge(ada_added, m + 1)
            if m + 2 < 6 * KT:
                load_ada(m + 2)

        if last_stage >= 3:
            pool.wait_ge(gate_done, 1)
            for h in range(NH):
                if h >= 2:
                    pool.wait_ge(shifted, h - 1)
                pool.tensor_scalar(bias_h[:, h % 2, :], dist[:, :], SLOPES[h], None, ALU.mult).then_inc(bias_made, 1)
        if last_stage >= 5:
            pool.wait_ge(ada_summed, 1)
            const(pool.memset(comb[:, :, :], 0.0))
            for i, r in ((0, 4), (1, 16)):
                v = comb[0:r, i, :].rearrange("p (m j) -> p m j", j=r)
                const(pool.affine_select(out=v, in_=v, compare_op=ALU.not_equal, fill=1.0, base=0,
                                         pattern=[[0, T // r], [-1, r]], channel_multiplier=1))
            assert made[0] == c_comb
            const(pool.memset(dil_mask[:, :], 1.0))
            band = dil_mask[:, 0:256]
            const(pool.affine_select(out=band, in_=band, compare_op=ALU.is_ge, fill=0.0, base=0,
                                     pattern=[[1, 256]], channel_multiplier=-1))
            pool.wait_ge(comb_done, 2)
            const(pool.tensor_tensor(dil_count[:, :], dil_count[:, :], dil_mask[:, :], ALU.add))
            for a, lo, w in ((1, 0, 256), (0, 256, 128)):
                v = dil_count[:, lo:lo + w]
                const(pool.affine_select(out=v, in_=v, compare_op=ALU.is_ge, fill=0.0, base=P * a,
                                         pattern=[[-1, w]], channel_multiplier=1))
            const(pool.tensor_scalar(dil_mask[:, :], dil_count[:, :], 0.5, NEG, ALU.is_lt, ALU.mult))
            assert made[0] == c_dil

    @block.scalar
    def _(act):
        def split_g(g):
            if g >= glimit:
                return
            c = CHUNK_OF[g]
            act.wait_ge(g_loaded[c % 2], 32 * (c // 2 + 1))
            if g >= 2:
                act.wait_ge(g_done, g - 1)
            paired = CHUNKS[c][0] == "pair"
            act.activation(part_view(g_hi, g, paired), raw_step(g), ACT.Copy).then_inc(g_hi_made, 1)

        def gained_hi(n, j, buf, signal, gain, first=0):
            piece_ready(act, n, j)
            for k in (2 * j, 2 * j + 1):
                act.activation(buf[:, k, :], xres[:, k, :], ACT.Identity, scale=par_col(gain, first + k)).then_inc(signal, 1)

        def squares(n, j):
            piece_ready(act, n, j)
            act.activation(ybuf[:, 2 * j:2 * j + 2, :], xres[:, 2 * j:2 * j + 2, :], ACT.Square).then_inc(sq_made, 1)

        def root(n):
            act.wait_ge(ss_done, n + 1)
            e = 1 if n == 6 else 0
            act.activation(rstd[:, :], ps[:, 0, 0:T], ACT.Sqrt, scale=1.0 / D, bias=eps[:, e:e + 1]).then_inc(rms_made, 1)

        def product_and_gained(first, n, buf, signal, gain, gain_first):
            for s in range(5):
                if s < 4:
                    act.wait_ge(g_done, first + s + 1)
                if s < 3:
                    split_g(first + s + 2)
                if s >= 1:
                    gained_hi(n, s - 1, buf, signal, gain, gain_first)
                if 1 <= s < 4:
                    squares(n, s - 1)
            squares(n, 3)
            split_g(first + 5)

        def hi_of_y(fills):
            for buf, signal, y0, bias in fills:
                for k in range(KT):
                    act.wait_ge(y_made, y0 + k + 1)
                    if bias is None:
                        act.activation(buf[:, k, :], ybuf[:, k, :], ACT.Copy).then_inc(signal, 1)
                    else:
                        act.activation(buf[:, k, :], ybuf[:, k, :], ACT.Identity, bias=mod_col(bias + k)).then_inc(signal, 1)

        def split_d(dslot, slot, loaded, free, j):
            act.wait_ge(d_loaded[slot], loaded)
            if free is not None:
                act.wait_ge(d_done, free)
            act.activation(d_hi[:, dslot, :], d_raw[:, slot, j, :], ACT.Copy).then_inc(d_hi_made, 1)

        def ffn(f):
            g0, d0, c0, dc0 = FFNS[f], FT * f, CHUNK_OF[FFNS[f]], FT // 2 * f

            def step(i, r, tail=False, first=False):
                s4 = i * 4
                g = gu[:, r % 2, 0, :]
                if f < 2:
                    act.wait_ge(gu_made, s4 + (d0 + r + 1))
                    act.activation(g, g, ACT.Silu).then_inc(silu_made, 1)
                else:
                    act.wait_ge(g_done, s4 + (g0 + r + 1))
                    act.activation(g, ps[:, gbank(g0 + r), 0:T], ACT.Silu).then_inc(silu_made, 1)
                act.wait_ge(hid_made, s4 + (d0 + r + 1))
                if not first or d0 + r >= 2:
                    act.wait_ge(d_done, s4 + (d0 + r - 1))
                act.activation(hid_hi[:, r % 2, :], gu[:, r % 2, 1, :], ACT.Copy).then_inc(hid_hi_made, 1)
                if tail:
                    split_g(g0 + 20 + r + 2)
                else:
                    c = c0 + (r + 2) // 2
                    act.wait_ge(g_loaded[c % 2], i * 32 + 32 * (c // 2 + 1))
                    act.wait_ge(g_done, s4 + (g0 + r + 1))
                    act.activation(part_view(g_hi, g0 + r, True), raw_cols(c % 2, r % 2, True),
                                   ACT.Copy).then_inc(g_hi_made, 1)
                if not (tail and r == 1):
                    c = dc0 + (r + 1) // 2
                    free = None if first and d0 + r == 0 else s4 + (d0 + r)
                    split_d((r + 1) % 2, c % 2, i * 16 + 16 * (c // 2 + 1), free, (r + 1) % 2)

            if f < 2:
                split_d(0, dc0 % 2, 16 * (dc0 // 2 + 1), None, 0)
                root(1 if f == 0 else 3)
            else:
                root(6)
                split_g(F2 + 1)
                hi_of_y([(opa_hi, opa_hi_made, Y_BASE[6], 24)])
                split_d(0, dc0 % 2, 16 * (dc0 // 2 + 1), None, 0)
            for r in range(4):
                step(0, r, first=True)
            with act.Fori(1, 5) as i:
                for r in range(4):
                    step(i, r)
            for r in range(2):
                step(5, r, tail=True)

        act.dma_start(token_view(ybuf), t["x"][0].rearrange("(a p) d -> p a d", p=P)).then_inc(x_loaded, 16)
        load_params(act, 0)
        act.dma_start(qg_raw[:, :, :], by_tile(t["b_w_qg"][0])[:, :, D:D + 48]).then_inc(side_loaded, 16)
        act.dma_start(if_raw[:, :, :], by_tile(t["w_in_2"][0])[:, :, 3584:3592]).then_inc(side_loaded, 16)
        for i, name in enumerate(("b_igate_2", "b_fgate_2")):
            act.dma_start(if_bias[:, i:i + 1], t[name].rearrange("a n -> n a")).then_inc(side_loaded, 16)
        act.wait_ge(consts, c_basic)
        split_g(0)
        act.wait_ge(par_made, 1)
        for j in range(4):
            gained_hi(0, j, opa_hi, opa_hi_made, "a_norm")
        split_g(1)
        for j in range(4):
            squares(0, j)
        act.wait_ge(side_loaded, 64)
        act.activation(qg_hi[:, :, :], qg_raw[:, :, :], ACT.Copy).then_inc(side_hi, 1)
        act.activation(if_hi[:, :, :], if_raw[:, :, :], ACT.Copy).then_inc(side_hi, 1)

        root(0)
        act.activation(csil[:, :], par_col("c_2", 0, 8), ACT.Silu).then_inc(csil_made, 1)
        for i in range(8):
            act.wait_ge(g_done, CV + i + 1)
            if i >= 2:
                act.wait_ge(g_evac, i - 1)
            act.activation(gu[:, i % 2, 0, :], ps[:, gbank(CV + i), 0:T], ACT.Copy).then_inc(c_copied, 1)
            split_g(CV + i + 2)
        for s in range(4):
            split_g(BG + s + 2)
            act.wait_ge(g_evac, BG + s + 1)
            act.activation(opb_hi[:, 2 * s:2 * s + 2, :], ybuf[:, 2 * s:2 * s + 2, :], ACT.Copy).then_inc(opb_hi_made, 1)
        product_and_gained(AO, 1, opa_hi, opa_hi_made, "f_norm", 0)
        if last_stage >= 2:
            ffn(0)

        if last_stage >= 3:
            for j in range(4):
                gained_hi(2, j, opa_hi, opa_hi_made, "kv_norm")
            for j in range(4):
                squares(2, j)
            for j in range(4):
                gained_hi(2, j, opb_hi, opb_hi_made, "b_norm")
            root(2)
            for s in range(6):
                act.wait_ge(g_done, KV + s + 1)
                split_g(KV + s + 2)
                act.wait_ge(g_evac, evacs(KV + s))
                tiles = kv_tiles(s)
                if s < 2:
                    act.wait_ge(pad_made, 2)
                    x = x_cmp[:, s, :, :].rearrange("p (t two) n -> p t two n", two=2)
                    act.activation(x[0:HD, :, 0, 0:T], tiles[0:HD], ACT.Copy)
                    act.activation(x[HD:P, :, 0, 0:T - 1], tiles[0:HD, :, 1:T], ACT.Copy).then_inc(kv_copied, 1)
                elif s in (2, 4):
                    k = k_dup[:, (s - 2) // 2, :, :].rearrange("p (t two) n -> p t two n", two=2)
                    act.activation(k[0:HD, :, 0, :], tiles[0:HD], ACT.Copy)
                    act.activation(k[HD:P, :, 0, :], tiles[0:HD], ACT.Copy).then_inc(kv_copied, 1)
            for s in range(2):
                act.wait_ge(g_done, QG + s + 1)
                split_g(QG + s + 2)
            act.wait_ge(cmp_hid_done, 1)
            act.activation(hid_cmp[:, 0, :, :, :].rearrange("p a g n -> p (a g n)"), ps[:, 0, 0:128],
                           ACT.Silu).then_inc(cmp_hid_silu, 1)
            act.wait_ge(cmp_hid_done, 2)
            for a in range(2):
                src = ps[:, 1, a * 64:(a + 1) * 64].rearrange("p (g n) -> p g n", g=NG)
                act.activation(vrep[:, a, :].rearrange("p (g h n) -> p g h n", g=NG, h=4),
                               src.unsqueeze(2).to_broadcast([P, NG, 4, 16]), ACT.Silu).then_inc(cmp_hid_silu, 1)
            act.wait_ge(gate_scaled, 1)
            act.activation(gate_row, gate_row, ACT.Exp, scale=-1.0).then_inc(gate_exp, 1)
            split_g(WO)
            split_g(WO + 1)
            act.wait_ge(cs_shift, 1)
            act.activation(ctmp, ctmp, ACT.Exp).then_inc(cs_exp, 1)
            act.wait_ge(pct_done, 1)
            act.activation(pct[:, :, :].rearrange("p a n -> p (a n)"), ps[:, 7, :], ACT.Copy).then_inc(pct_made, 1)
            for h in range(NH + 4):
                if h >= 5 and h % 2 == 1:
                    j = (h - 5) // 2
                    act.wait_ge(pv_done, 2 * j + 2)
                    act.activation(opa_hi[:, j, :], ps[:, 6 + j % 2, 0:T], ACT.Copy).then_inc(opa_hi_made, 1)
                if 2 <= h < NH + 2:
                    act.wait_ge(pt_done, h - 1)
                    act.activation(pt_buf[:, 0, :], ps[:, 4, 0:384], ACT.Copy).then_inc(pt_slc, 1)
                if h < NH:
                    act.wait_ge(shifted, h + 1)
                    for a, b, lo, w in ((1, 0, 0, 256), (1, 1, 256, 256), (0, 0, 512, 128), (0, 1, 640, 128)):
                        e = e_buf[:, h % 3, lo:lo + w]
                        i = 2 * a + b
                        last = act.activation(e, e, ACT.Exp, bias=nmax[:, h % 3, i:i + 1], scale=-1.0,
                                              accum_out=zsum[:, h % 3, i:i + 1])
                    last.then_inc(exp_made, 1)
            product_and_gained(WO, 3, opb_hi, opb_hi_made, "f_norm", 8)
        if last_stage >= 4:
            ffn(1)

        if last_stage >= 5:
            for j in range(4):
                squares(4, j)
                for k in (2 * j, 2 * j + 1):
                    ins = act.activation(qk_m[:, k, :], xres[:, k, :], ACT.Square, scale=par_col("final_norm", k))
                ins.then_inc(sqg_made, 1)
            act.wait_ge(ms_made, 1)
            act.activation(rstd[:, :], rstd[:, :], ACT.Sqrt).then_inc(rms_made, 1)
            act.activation(r_next, r_next, ACT.Sqrt, bias=eps[:, 1:2]).then_inc(rms_made, 1)
            hi_of_y([(opa_hi, opa_hi_made, Y_BASE[5], 0)])
            for s in range(14):
                g = MX + s
                act.wait_ge(g_done, g + 1)
                if MX_QM <= g < MX_VM:
                    n = g - MX_QM
                    if n >= 1:
                        act.wait_ge(conv_made, n)
                    act.activation(zpad[:, :, 4:T + 4], pair(gbank(g)), ACT.Copy).then_inc(z_copied, 1)
                split_g(g + 2)
                if s < 4:
                    act.wait_ge(g_evac, evacs(g))
                    act.activation(ybuf[:, 2 * s:2 * s + 2, :], qk_a[:, 2 * s:2 * s + 2, :], ACT.Square).then_inc(qk_sq, 1)
                if s == 1:
                    act.wait_ge(if_in, 2)
                    act.activation(rows[:, 5, :], rows[:, 1, :], ACT.Abs).then_inc(if_abs, 1)
                    act.wait_ge(if_abs, 1)
                    act.activation(rows[:, 5, :], rows[:, 5, :], ACT.Exp, scale=-1.0).then_inc(if_abs, 1)
                if s == 2:
                    act.wait_ge(if_abs, 2)
                    act.activation(rows[:, 5, :], rows[:, 5, :], ACT.Ln, bias=1.0).then_inc(if_abs, 1)
                if 2 <= s < 6:
                    j = s - 2
                    act.wait_ge(qk_ss, j + 1)
                    act.activation(ybuf[:, 2 * j:2 * j + 2, :], pair(j % 2), ACT.Ln, scale=1.0 / HD,
                                   bias=eps[:, 1:2]).then_inc(qk_root, 1)
                if s == 5:
                    act.wait_ge(qk_root, 4)
                    for j in range(4):
                        y = ybuf[:, 2 * j:2 * j + 2, :]
                        act.activation(y, y, ACT.Exp, scale=-0.5).then_inc(qk_root, 1)
                if MX_QM <= g < MX_VM:
                    act.wait_ge(conv_made, n + 1)
                    m = qk_m[:, 2 * n:2 * n + 2, :]
                    act.activation(m, m, ACT.Silu).then_inc(conv_ready_made, 1)
                if g >= MX_OG:
                    n = g - MX_OG
                    act.activation(og_s[:, 2 * n:2 * n + 2, :], pair(gbank(g)), ACT.Sigmoid).then_inc(og_made, 1)

        if last_stage >= 6:
            for h in range(NH2 + 4):
                if h >= 5 and h % 2 == 1:
                    j = (h - 5) // 2
                    act.wait_ge(pv_done, NH + 2 * j + 2)
                    act.activation(opa_hi[:, j, :], ps[:, 6 + j % 2, 0:T], ACT.Copy).then_inc(opa_hi_made, 1)
                if 2 <= h < NH2 + 2:
                    act.wait_ge(pt_done, NH + h - 1)
                    act.activation(pt_dil[:, h % 2, :], ps[:, 4 + h % 2, 0:384], ACT.Copy).then_inc(pt_slc, 1)
                if h < NH2:
                    act.wait_ge(shifted, NH + h + 1)
                    for a, lo, w in ((1, 0, 256), (0, 256, 128)):
                        e = e_dil[:, h % 3, lo:lo + w]
                        last = act.activation(e, e, ACT.Exp, bias=nmax[:, h % 3, a:a + 1], scale=-1.0)
                    last.then_inc(exp_made, 1)
            for m in range(NM):
                act.wait_ge(arg_made, m + 1)
                act.activation(l_emt[:, m, :], ps[:, m, T:2 * T], ACT.Exp, scale=-1.0).then_inc(emt_made, 1)
                act.activation(decay[:, m, 0:256], decay[:, m, 0:256], ACT.Exp, bias=a_col[:, 0, m:m + 1])
                act.activation(decay[:, m, 256:384], decay[:, m, 256:384], ACT.Exp,
                               bias=a_col[:, 1, m:m + 1]).then_inc(decay_made, 1)
            for m in range(NM):
                act.wait_ge(num_done, m + 1)
                act.activation(l_abs[:, m, :], ps[:, m, T:2 * T], ACT.Abs).then_inc(abs_made, 1)
                if m >= 1:
                    act.wait_ge(num_made, m)
                    act.activation(l_sq[:, m - 1, :], mix[:, 3 + m, :], ACT.Square).then_inc(lsq_made, 1)
            act.wait_ge(num_made, NM)
            act.activation(l_sq[:, NM - 1, :], mix[:, 3 + NM, :], ACT.Square).then_inc(lsq_made, 1)
            act.wait_ge(lss_done, NM)
            act.activation(mix[:, 0:4, :], ps[:, 0:4, 0:T], ACT.Ln, scale=1.0 / P, bias=eps[:, 1:2]).then_inc(lroot_made, 1)
            act.wait_ge(lroot_made, 1)
            for m in range(NM):
                act.activation(mix[:, m, :], mix[:, m, :], ACT.Exp, scale=-0.5).then_inc(lroot_made, 1)
            for m in range(NM):
                act.wait_ge(mix_made, m + 1)
                act.activation(opa_hi[:, 4 + m, :], mix[:, 4 + m, :], ACT.Copy).then_inc(opa_hi_made, 1)
            for s in range(4):
                act.wait_ge(g_done, MO + s + 1)
                if s < 3:
                    split_g(MO + s + 2)
                if s >= 1:
                    squares(6, s - 1)
            squares(6, 3)
        if last_stage >= 7:
            ffn(2)

    @block.vector
    def _(dve):
        links = [0]

        def own(ins):
            links[0] += 1
            ins.then_inc(dve_own, 1)
            dve.wait_ge(dve_own, links[0])

        def split_g(g):
            if g >= glimit:
                return
            paired = CHUNKS[CHUNK_OF[g]][0] == "pair"
            dve.wait_ge(g_hi_made, g + 1)
            dve.tensor_tensor(part_view(g_lo, g, paired), raw_step(g), part_view(g_hi, g, paired).bitcast(F32),
                              ALU.subtract).then_inc(g_lo_made, 1)

        def add_squares(n, pieces=(1, 2, 3)):
            buf = qk_m if n == 5 else ybuf
            for j in pieces:
                if n == 5:
                    dve.wait_ge(sqg_made, j + 1)
                else:
                    dve.wait_ge(sq_made, 4 * (n if n < 5 else 5) + j + 1)
                ins = dve.tensor_tensor(buf[:, 0:2, :], buf[:, 0:2, :], buf[:, 2 * j:2 * j + 2, :], ALU.add)
                if j < 3:
                    own(ins)
                else:
                    ins.then_inc(sq_added, 1)

        def norm_parts(scale, fills):
            for hi, lo, hi_signal, hi0, lo_signal, gain, bias in fills:
                def make_y(k):
                    dve.scalar_tensor_tensor(out=ybuf[:, k, :], in0=xres[:, k, :], scalar=gain(k), in1=scale,
                                             op0=ALU.mult, op1=ALU.mult).then_inc(y_made, 1)
                make_y(0)
                make_y(1)
                for k in range(KT):
                    if k + 2 < KT:
                        make_y(k + 2)
                    dve.wait_ge(hi_signal, hi0 + k + 1)
                    h = hi[:, k, :].bitcast(F32)
                    if bias is None:
                        ins = dve.tensor_tensor(lo[:, k, :], ybuf[:, k, :], h, ALU.subtract)
                    else:
                        ins = dve.scalar_tensor_tensor(out=lo[:, k, :], in0=ybuf[:, k, :], scalar=mod_col(bias + k),
                                                       in1=h, op0=ALU.add, op1=ALU.subtract)
                    ins.then_inc(lo_signal, 1)

        def gained_lo(j, hi, lo, hi_signal, hi0, lo_signal, gain, first=0):
            for k in (2 * j, 2 * j + 1):
                dve.wait_ge(hi_signal, hi0 + k + 1)
                dve.scalar_tensor_tensor(out=lo[:, k, :], in0=xres[:, k, :], scalar=par_col(gain, first + k),
                                         in1=hi[:, k, :].bitcast(F32), op0=ALU.mult,
                                         op1=ALU.subtract).then_inc(lo_signal, 1)

        def invert_rms(n):
            dve.wait_ge(rms_made, n + 1)
            own(dve.reciprocal(rstd[:, :], rstd[:, :]))

        def fill_a(fill, gain, bias=None):
            return (opa_hi, opa_lo, opa_hi_made, 8 * A_FILL[fill], opa_made, gain, bias)

        def split_d(dslot, slot, n, j):
            dve.wait_ge(d_hi_made, n)
            dve.tensor_tensor(d_lo[:, dslot, :], d_raw[:, slot, j, :], d_hi[:, dslot, :].bitcast(F32),
                              ALU.subtract).then_inc(d_lo_made, 1)

        def ffn(f, norm, fill=None, gain=None, bias=None):
            g0, d0, c0, dc0 = FFNS[f], FT * f, CHUNK_OF[FFNS[f]], FT // 2 * f

            def step(i, r, tail):
                s4 = i * 4
                g, u = gu[:, r % 2, 0, :], gu[:, r % 2, 1, :]
                if f < 2:
                    dve.wait_ge(g_done, s4 + (g0 + r + 1))
                    dve.tensor_tensor(gu[:, r % 2, :, :], pair(gbank(g0 + r)),
                                      rstd[:, :].unsqueeze(1).to_broadcast([P, 2, T]), ALU.mult).then_inc(gu_made, 1)
                    dve.wait_ge(gu_made, s4 + (d0 + r + 1))
                    dve.wait_ge(silu_made, s4 + (d0 + r + 1))
                    dve.tensor_tensor(u, g, u, ALU.mult).then_inc(hid_made, 1)
                else:
                    dve.wait_ge(silu_made, s4 + (d0 + r + 1))
                    dve.tensor_tensor(u, g, ps[:, gbank(g0 + r), T:2 * T], ALU.mult).then_inc(hid_made, 1)
                dve.wait_ge(hid_hi_made, s4 + (d0 + r + 1))
                dve.tensor_tensor(hid_lo[:, r % 2, :], u, hid_hi[:, r % 2, :].bitcast(F32),
                                  ALU.subtract).then_inc(hid_lo_made, 1)
                if tail:
                    if r == 0:
                        split_g(g0 + 22)
                else:
                    c = c0 + (r + 2) // 2
                    dve.wait_ge(g_hi_made, s4 + (g0 + r + 3))
                    dve.tensor_tensor(part_view(g_lo, g0 + r, True), raw_cols(c % 2, r % 2, True),
                                      part_view(g_hi, g0 + r, True).bitcast(F32), ALU.subtract).then_inc(g_lo_made, 1)
                if not (tail and r == 1):
                    c = dc0 + (r + 1) // 2
                    split_d((r + 1) % 2, c % 2, s4 + (d0 + r + 2), (r + 1) % 2)

            if f < 2:
                split_d(0, dc0 % 2, d0 + 1, 0)
                invert_rms(norm)
            else:
                invert_rms(norm)
                norm_parts(rstd[:, :], [fill_a(fill, gain, bias)])
                split_g(F2 + 1)
                split_d(0, dc0 % 2, d0 + 1, 0)
            if f == 1:
                dve.wait_ge(ada_summed, 1)
                own(dve.tensor_tensor(mod[:, :], ps[:, 1, 0:48], par_col("b_ada_2", 0, 48), ALU.add))
                dve.scalar_tensor_tensor(out=gmod[:, 0:8], in0=mod[:, 8:16], scalar=1.0, in1=par_col("g_mix_2", 0, 8),
                                         op0=ALU.add, op1=ALU.mult).then_inc(mod_made, 1)
                dve.scalar_tensor_tensor(out=gmod[:, 8:16], in0=mod[:, 32:40], scalar=1.0, in1=par_col("g_ffn_2", 0, 8),
                                         op0=ALU.add, op1=ALU.mult).then_inc(mod_made, 1)
                dve.wait_ge(mod_made, 2)
                own(dve.tensor_tensor(gmod[:, 0:8], gmod[:, 0:8], par_col("final_norm", 0, 8), ALU.mult))
                own(dve.tensor_scalar(q_gain, par_col("q_norm_g_2"), HD ** -0.5, None, ALU.mult))
            with dve.Fori(0, 5) as i:
                for r in range(4):
                    step(i, r, False)
            for r in range(2):
                step(5, r, True)
            dve.wait_ge(d_done, d0 + FT)
            for j in range(4):
                if f < 2:
                    x = xres[:, 2 * j:2 * j + 2, :]
                    dve.tensor_tensor(x, pair(j), x, ALU.add).then_inc(res_added, 1)
                    continue
                for k in (2 * j, 2 * j + 1):
                    ins = dve.scalar_tensor_tensor(out=xres[:, k, :], in0=pair(j)[:, k % 2, :], scalar=mod_col(40 + k),
                                                   in1=xres[:, k, :], op0=ALU.mult, op1=ALU.add)
                ins.then_inc(res_added, 1)

        def evac(ins, g):
            ins.then_inc(g_evac, 1)
            dve.wait_ge(g_evac, evacs(g))

        for j in range(4):
            dve.wait_ge(x_turned, j + 1)
            dve.tensor_copy(xres[:, 2 * j:2 * j + 2, :], pair(j)).then_inc(xres_made, 1)
        dve.wait_ge(par_turned, 1)
        dve.tensor_copy(par[:, :], ps[:, 4, 0:NROWS]).then_inc(par_made, 1)
        dve.wait_ge(par_made, 1)
        split_g(0)
        for j in range(4):
            gained_lo(j, opa_hi, opa_lo, opa_hi_made, 0, opa_made, "a_norm")
        split_g(1)
        for n, (hi, lo, raw) in enumerate(((qg_hi, qg_lo, qg_raw), (if_hi, if_lo, if_raw))):
            dve.wait_ge(side_hi, n + 1)
            dve.tensor_tensor(lo[:, :, :], raw[:, :, :], hi[:, :, :].bitcast(F32), ALU.subtract).then_inc(side_lo, 1)

        add_squares(0)
        invert_rms(0)
        own(dve.tensor_tensor(r_sq, rstd[:, :], rstd[:, :], ALU.mult))
        for i in range(8):
            g = CV + i
            dve.wait_ge(c_copied, i + 1)
            z, u = zpad[:, i % 2, :], ybuf[:, i, :]
            evac(dve.tensor_tensor(z[:, 4:T + 4], ps[:, gbank(g), T:2 * T], gu[:, i % 2, 0, :], ALU.mult), g)
            own(dve.tensor_tensor(z[:, 4:T + 4], z[:, 4:T + 4], r_sq, ALU.mult))
            own(dve.tensor_scalar(u, z[:, 2:T + 2], par_col("a_conv", i), None, ALU.mult))
            for w in (1, 2):
                own(dve.scalar_tensor_tensor(out=u, in0=z[:, 2 + w:T + 2 + w], scalar=par_col("a_conv", 8 * w + i),
                                             in1=u, op0=ALU.mult, op1=ALU.add))
            split_g(g + 2)
        for s in range(4):
            y = ybuf[:, 2 * s:2 * s + 2, :]
            own(dve.tensor_tensor(y, y, rstd[:, :].unsqueeze(1).to_broadcast([P, 2, T]), ALU.mult))
            dve.wait_ge(g_done, BG + s + 1)
            evac(dve.tensor_tensor(y, pair(gbank(BG + s)), y, ALU.mult), BG + s)
            split_g(BG + s + 2)
            dve.wait_ge(opb_hi_made, s + 1)
            dve.tensor_tensor(opb_lo[:, 2 * s:2 * s + 2, :], y, opb_hi[:, 2 * s:2 * s + 2, :].bitcast(F32),
                              ALU.subtract).then_inc(opb_made, 1)

        def add_product(first, *operand):
            hi, lo, hi_signal, hi0, lo_signal, gain, gain_first = operand
            for s in range(5):
                if s < 4:
                    dve.wait_ge(g_done, first + s + 1)
                    x = xres[:, 2 * s:2 * s + 2, :]
                    evac(dve.tensor_tensor(x, pair(gbank(first + s)), x, ALU.add), first + s)
                if s < 3:
                    split_g(first + s + 2)
                if s >= 1:
                    gained_lo(s - 1, hi, lo, hi_signal, hi0, lo_signal, gain, gain_first)
            add_squares(1 if first == AO else 3)
            split_g(first + 5)

        add_product(AO, opa_hi, opa_lo, opa_hi_made, 8 * A_FILL["n1"], opa_made, "f_norm", 0)
        if last_stage >= 2:
            ffn(0, 1)

        if last_stage >= 3:
            dve.memset(kc_blk[:, :, :, :], 0.0).then_inc(kc_zeroed, 1)
            dve.memset(x_cmp[:, :, :, 256:288], 0.0).then_inc(pad_made, 1)
            dve.memset(x_cmp[HD:P, :, :, 255:256], 0.0).then_inc(pad_made, 1)
            for j in range(4):
                gained_lo(j, opa_hi, opa_lo, opa_hi_made, 8 * A_FILL["n2"], opa_made, "kv_norm")
            add_squares(2)
            split_g(KV + 1)
            invert_rms(2)
            r_both = rstd[:, :].unsqueeze(1).to_broadcast([P, 2, T])

            def cmp_blocks(w):
                pe = par_col("cmp_pe_v" if w else "cmp_pe_k", 0, 16)
                for q in range(2):
                    x = x_cmp[:, w, :, 16 * q:16 * q + 256].rearrange("p g (n l two) -> p l g n two", l=8, two=2)
                    e = pe[:, 8 * q:8 * q + 8].unsqueeze(2).unsqueeze(3).to_broadcast([P, 8, NG, 16])
                    dve.tensor_tensor(b_cmp[:, 8 * q:8 * q + 8, :, :], x[:, :, :, :, 0], e, ALU.add).then_inc(b_cmp_made, 1)

            for s in range(6):
                g = KV + s
                dve.wait_ge(g_done, g + 1)
                tiles = pair(gbank(g))
                if s in (3, 5):
                    if s == 3:
                        dve.wait_ge(r_turned, 1)
                        own(dve.tensor_copy(r_col, ps[:, 1, 0:2 * P].rearrange("p (a n) -> p a n", a=TT)[:, :, 0]))
                    v = v_tok[:, (s - 3) // 2, :, :]
                    dve.tensor_scalar(v[:, 0, :], tiles[:, 0, :], r_col[:, 0:1], None, ALU.mult)
                    evac(dve.tensor_scalar(v[:, 1, :], tiles[:, 1, :], r_col[:, 1:2], None, ALU.mult), g)
                else:
                    if s >= 2:
                        dve.wait_ge(kv_copied, 2)
                    kv = kv_tiles(s)
                    evac(dve.tensor_tensor(kv, tiles, r_both, ALU.mult), g)
                    if s < 2:
                        x = x_cmp[:, s, :, :].rearrange("p (t two) n -> p t two n", two=2)
                        dve.tensor_copy(x[0:HD, :, 1, 0:T], kv[HD:P])
                        own(dve.tensor_copy(x[HD:P, :, 1, 0:T - 1], kv[HD:P, :, 1:T]))
                    else:
                        k = k_dup[:, (s - 2) // 2, :, :].rearrange("p (t two) n -> p t two n", two=2)
                        dve.tensor_copy(k[0:HD, :, 1, :], kv[HD:P])
                        dve.tensor_copy(k[HD:P, :, 1, :], kv[HD:P]).then_inc(k_copied, 1)
                split_g(g + 2)
                if s == 0:
                    dve.wait_ge(kv_copied, 1)
                    cmp_blocks(0)
                if s < 4:
                    gained_lo(s, opb_hi, opb_lo, opb_hi_made, B_FILL["b"], opb_made, "b_norm")
            for s in range(4):
                g = QG + s
                dve.wait_ge(g_done, g + 1)
                evac(dve.scalar_tensor_tensor(out=q_t[:, 2 * s:2 * s + 2, :], in0=pair(gbank(g)), scalar=HD ** -0.5,
                                              in1=r_both, op0=ALU.mult, op1=ALU.mult), g)
                if s < 2:
                    split_g(g + 2)
            dve.wait_ge(kv_copied, 4)
            dve.wait_ge(gate_done, 1)
            dve.tensor_tensor(gate_row, ps[0:48, 3, 0:T], rstd[0:48, :], ALU.mult).then_inc(gate_scaled, 1)
            dve.wait_ge(cmp_hid_done, 1)
            cmp_blocks(1)
            dve.wait_ge(gate_turned, 1)
            own(dve.tensor_copy(gates[:, :, :], ps[:, 3, 256:352].rearrange("p (a n) -> p a n", a=TT)))
            own(dve.tensor_scalar(gates[:, :, :], gates[:, :, :], 1.0, None, ALU.add))
            dve.reciprocal(gates[:, :, :], gates[:, :, :]).then_inc(gates_made, 1)
            dve.wait_ge(kc_done, 1)
            dve.wait_ge(consts, c_block1)
            dve.wait_ge(kc_zeroed, 1)
            for b in range(2):
                dve.tensor_copy(kc_blk[HD * b:HD * b + HD, :, b, :],
                                ps[HD * b:HD * b + HD, 2, 0:64].rearrange("p (g n) -> p g n", g=NG)).then_inc(kc_made, 1)
            for half in range(2):
                v = ps[:, 2, HD * (1 + half):HD * (2 + half)].unsqueeze(1).to_broadcast([P, 8, HD])
                dve.tensor_tensor(vc_blk[:, 8 * half:8 * half + 8, :], v, blk16.unsqueeze(2).to_broadcast([P, 8, HD]),
                                  ALU.mult).then_inc(kc_made, 1)
            split_g(WO)
            split_g(WO + 1)
            dve.wait_ge(cs_done, 1)
            own(dve.tensor_tensor(ctmp, ps[:, 4, :], cmp_bias[:, :, :, :].rearrange("p a h n -> p (a h n)"), ALU.add))
            own(dve.tensor_reduce(cmax, c4(ctmp), AX_X, ALU.max))
            dve.tensor_tensor(c4(ctmp), c4(ctmp), cmax.unsqueeze(2).to_broadcast([P, 32, 16]),
                              ALU.subtract).then_inc(cs_shift, 1)
            dve.wait_ge(cs_exp, 1)
            own(dve.tensor_reduce(cmax, c4(ctmp), AX_X, ALU.add))
            own(dve.reciprocal(cmax, cmax))
            dve.wait_ge(gates_made, 1)
            gate0 = gates[:, :, :].rearrange("p a (h b) -> p a h b", b=3)[:, :, :, 0]
            own(dve.tensor_tensor(cfac[:, :, :], cmax.rearrange("p (a h) -> p a h", a=TT), gate0, ALU.mult))
            own(dve.tensor_tensor(cfac[:, :, :], cfac[:, :, :], any_vis[:, :].unsqueeze(2).to_broadcast([P, TT, NH]),
                                  ALU.mult))
            f = cfac[:, :, :].rearrange("p a h -> p (a h)")
            dve.tensor_tensor(c4(ctmp), c4(ctmp), f.unsqueeze(2).to_broadcast([P, 32, 16]), ALU.mult).then_inc(cs_made, 1)
            for h in range(NH + 4):
                if 2 <= h < NH + 2:
                    p = h - 2
                    dve.wait_ge(exp_made, p + 1)
                    own(dve.reciprocal(fac[:, p % 3, :], zsum[:, p % 3, :]))
                    g2 = gates[:, :, 3 * p + 1:3 * p + 3]
                    f4 = fac[:, p % 3, :].rearrange("p (a b) -> p a b", a=TT)
                    own(dve.tensor_tensor(f4, f4, g2, ALU.mult))
                    for a, b, lo, w in ((1, 0, 0, 256), (1, 1, 256, 256), (0, 0, 512, 128), (0, 1, 640, 128)):
                        e = e_buf[:, p % 3, lo:lo + w]
                        i = 2 * a + b
                        last = dve.tensor_scalar(e, e, fac[:, p % 3, i:i + 1], None, ALU.mult)
                    last.then_inc(scaled, 1)
                if h < NH:
                    dve.wait_ge(scored, h + 1)
                    dve.wait_ge(bias_made, h + 1)
                    for a, b, lo, w in ((1, 0, 0, 256), (1, 1, 256, 256), (0, 0, 512, 128), (0, 1, 640, 128)):
                        i = 2 * a + b
                        src = ps[:, 2 * (h % 2) + (1 - a), b * w:(b + 1) * w]
                        bias = bias_h[:, h % 2, 0:256] if a else bias_h[:, h % 2, 256:384]
                        last = dve.tensor_tensor_reduce(e_buf[:, h % 3, lo:lo + w], src, bias, -1.0, 3.0e38,
                                                        ALU.add, ALU.min, nmax[:, h % 3, i:i + 1])
                    last.then_inc(shifted, 1)
                if 2 <= h < NH + 2:
                    dve.wait_ge(pt_done, h - 1)
                    dve.tensor_copy(pt_buf[:, 1, :], ps[:, 5, 0:384]).then_inc(pt_win, 1)
                if h >= 5 and h % 2 == 1:
                    j = (h - 5) // 2
                    dve.wait_ge(opa_hi_made, 8 * A_FILL["attn"] + j + 1)
                    dve.tensor_tensor(opa_lo[:, j, :], ps[:, 6 + j % 2, 0:T], opa_hi[:, j, :].bitcast(F32),
                                      ALU.subtract).then_inc(opa_made, 1)
            add_product(WO, opb_hi, opb_lo, opb_hi_made, B_FILL["n3"], opb_made, "f_norm", 8)
        if last_stage >= 4:
            ffn(1, 3)

        if last_stage >= 5:
            add_squares(4)
            add_squares(5)
            split_g(MX + 1)
            dve.wait_ge(ss_done, 6)
            own(dve.tensor_scalar(rstd[:, :], ps[:, 0, 0:T], 1.0 / D, 1e-5, ALU.mult, ALU.add))
            own(dve.reciprocal(rstd[:, :], rstd[:, :]))
            dve.scalar_tensor_tensor(out=r_next, in0=ps[:, 0, T:2 * T], scalar=1.0 / D, in1=rstd[:, :],
                                     op0=ALU.mult, op1=ALU.mult).then_inc(ms_made, 1)
            dve.wait_ge(rms_made, 6)
            own(dve.reciprocal(r_next, r_next))
            own(dve.tensor_tensor(r_next, r_next, rstd[:, :], ALU.mult))
            norm_parts(r_next, [fill_a("n5", lambda k: gmod[:, k:k + 1], 0)])
            for k in range(KT):
                ins = dve.scalar_tensor_tensor(out=xres[:, k, :], in0=xres[:, k, :], scalar=par_col("final_norm", k),
                                               in1=rstd[:, :], op0=ALU.mult, op1=ALU.mult)
                if k % 2 == 1:
                    ins.then_inc(res_added, 1)
            dve.wait_ge(comb_done, 1)
            dve.tensor_copy(dil_count[:, :], ps[:, 1, 0:384]).then_inc(comb_done, 1)
            for s in range(14):
                g = MX + s
                dve.wait_ge(g_done, g + 1)
                tiles = pair(gbank(g))
                if g < MX_VA:
                    evac(dve.tensor_copy(qk_a[:, 2 * s:2 * s + 2, :], tiles), g)
                elif g < MX_QM:
                    n = g - MX_VA
                    evac(dve.tensor_copy(v_a[:, :, n * T:(n + 1) * T], tiles), g)
                elif g < MX_VM:
                    n = g - MX_QM
                    dve.wait_ge(z_copied, n + 1)
                    for a in range(2):
                        i, z = 2 * n + a, zpad[:, a, :]
                        u = qk_m[:, i, :]
                        ins = dve.tensor_scalar(u, z[:, 1:T + 1], par_col("w_conv_2", i), par_col("b_conv_2", i),
                                                ALU.mult, ALU.add)
                        if a == 0:
                            evac(ins, g)
                        else:
                            own(ins)
                        for w in (1, 2, 3):
                            ins = dve.scalar_tensor_tensor(out=u, in0=z[:, 1 + w:T + 1 + w],
                                                           scalar=par_col("w_conv_2", 8 * w + i), in1=u,
                                                           op0=ALU.mult, op1=ALU.add)
                            if w < 3:
                                own(ins)
                    ins.then_inc(conv_made, 1)
                elif g < MX_OG:
                    n = g - MX_VM
                    evac(dve.tensor_copy(v_m[:, :, n * T:(n + 1) * T], tiles), g)
                if s == 1:
                    dve.wait_ge(if_done, 1)
                    dve.wait_ge(side_loaded, 64)
                    for i in range(2):
                        dve.tensor_scalar(rows[:, i, :], ps[0:NM, 2, i * T:(i + 1) * T], if_bias[:, i:i + 1], None,
                                          ALU.add).then_inc(if_in, 1)
                if s < 13:
                    split_g(g + 2)
                if s == 4:
                    own(dve.memset(ones_row[:, :], 1.0))
                    dve.wait_ge(if_abs, 3)
                    own(dve.scalar_tensor_tensor(out=rows[:, 1, :], in0=rows[:, 1, :], scalar=0.0, in1=rows[:, 5, :],
                                                 op0=ALU.min, op1=ALU.subtract))
                    own(dve.tensor_tensor_scan(rows[:, 2, :], ones_row[:, :], rows[:, 1, :], 0.0, ALU.mult, ALU.add))
                    own(dve.tensor_tensor(rows[:, 3, :], rows[:, 0, :], rows[:, 2, :], ALU.subtract))
                    own(dve.tensor_tensor_scan(rows[:, 4, :], ones_row[:, :], rows[:, 3, :], 0.0, ALU.mult, ALU.max))
                    dve.tensor_scalar(rows[:, 5, :], rows[:, 4, :], -1.0, None, ALU.mult)
                    dve.tensor_tensor(rows[:, 6, :], rows[:, 2, :], rows[:, 4, :], ALU.add).then_inc(rows_made, 1)
                if s == 10:
                    dve.wait_ge(a_turned, 1)
                    dve.tensor_copy(a_col[:, :, :], ps[:, 2, 0:8].rearrange("p (a n) -> p a n", a=TT)).then_inc(a_made, 1)
                if s in (10, 11):
                    for j in (2 * s - 20, 2 * s - 19):
                        dve.wait_ge(qk_root, 5 + j)
                        for k in (2 * j, 2 * j + 1):
                            ins = dve.scalar_tensor_tensor(out=qk_a[:, k, :], in0=qk_a[:, k, :],
                                                           scalar=q_gain if k < 4 else par_col("k_norm_g_2"),
                                                           in1=ybuf[:, k, :], op0=ALU.mult, op1=ALU.mult)
                        ins.then_inc(qk_made, 1)

        if last_stage >= 6:
            for h in range(NH2 + 4):
                if 2 <= h < NH2 + 2:
                    p = h - 2
                    dve.wait_ge(exp_made, NH + p + 1)
                    for a, lo, w in ((1, 0, 256), (0, 256, 128)):
                        e = e_dil[:, p % 3, lo:lo + w]
                        last = dve.tensor_tensor_reduce(e, e, dil_count[:, lo:lo + w], 1.0, 0.0, ALU.mult, ALU.add,
                                                        zsum[:, p % 3, a:a + 1])
                    own(last)
                    own(dve.reciprocal(fac[:, p % 3, 0:2], zsum[:, p % 3, 0:2]))
                    for a, lo, w in ((1, 0, 256), (0, 256, 128)):
                        e = e_dil[:, p % 3, lo:lo + w]
                        last = dve.tensor_scalar(e, e, fac[:, p % 3, a:a + 1], None, ALU.mult)
                    last.then_inc(scaled, 1)
                if h < NH2:
                    dve.wait_ge(scored, NH + h + 1)
                    dve.wait_ge(consts, c_dil)
                    for a, lo, w in ((1, 0, 256), (0, 256, 128)):
                        last = dve.tensor_tensor_reduce(e_dil[:, h % 3, lo:lo + w], ps[:, h % 2, lo:lo + w],
                                                        dil_mask[:, lo:lo + w], -1.0, 3.0e38, ALU.add, ALU.min,
                                                        nmax[:, h % 3, a:a + 1])
                    last.then_inc(shifted, 1)
                if h == NH2 + 2:
                    split_g(MO + 1)
                if h >= 5 and h % 2 == 1:
                    j = (h - 5) // 2
                    dve.wait_ge(opa_hi_made, 8 * A_FILL["mix"] + j + 1)
                    dve.tensor_tensor(opa_lo[:, j, :], ps[:, 6 + j % 2, 0:T], opa_hi[:, j, :].bitcast(F32),
                                      ALU.subtract).then_inc(opa_made, 1)
            def lstm_weights(m):
                dve.wait_ge(ls_done, m + 1)
                dve.wait_ge(decay_made, m + 1)
                dve.scalar_tensor_tensor(out=decay[:, m, :], in0=ps[:, 4 + m, 0:384], scalar=P ** -0.5,
                                         in1=decay[:, m, :], op0=ALU.mult, op1=ALU.mult).then_inc(ls_made, 1)

            for m in range(NM):
                dve.wait_ge(m_cast, m + 1)
                dve.tensor_tensor(decay[:, m, 0:256], ps[:, m, 0:T], lstm_mask[:, 0:256], ALU.add)
                dve.tensor_tensor(decay[:, m, 256:384], ps[:, m, P:T], lstm_mask[:, 256:384], ALU.add).then_inc(arg_made, 1)
                if m >= 1:
                    lstm_weights(m - 1)
            lstm_weights(NM - 1)
            for m in range(NM):
                d = l_abs[:, m, :]
                dve.wait_ge(abs_made, m + 1)
                dve.wait_ge(emt_made, m + 1)
                own(dve.tensor_tensor(d, d, l_emt[:, m, :], ALU.max))
                own(dve.reciprocal(d, d))
                dve.tensor_tensor(mix[:, 4 + m, :], ps[:, m, 0:T], d, ALU.mult).then_inc(num_made, 1)
            for m in range(NM):
                dve.wait_ge(lroot_made, 2 + m)
                x = mix[:, 4 + m, :]
                own(dve.scalar_tensor_tensor(out=x, in0=x, scalar=par_col("mlstm_norm_g_2", m), in1=mix[:, m, :],
                                             op0=ALU.mult, op1=ALU.mult))
                dve.tensor_tensor(x, x, og_s[:, m, :], ALU.mult).then_inc(mix_made, 1)
                dve.wait_ge(opa_hi_made, 8 * A_FILL["mix"] + 5 + m)
                dve.tensor_tensor(opa_lo[:, 4 + m, :], x, opa_hi[:, 4 + m, :].bitcast(F32),
                                  ALU.subtract).then_inc(opa_made, 1)
            for s in range(4):
                dve.wait_ge(g_done, MO + s + 1)
                for a in range(2):
                    k = 2 * s + a
                    ins = dve.scalar_tensor_tensor(out=xres[:, k, :], in0=pair(gbank(MO + s))[:, a, :],
                                                   scalar=mod_col(16 + k), in1=xres[:, k, :],
                                                   op0=ALU.mult, op1=ALU.add)
                evac(ins, MO + s)
                if s < 3:
                    split_g(MO + s + 2)
                if s >= 2:
                    add_squares(6, (s - 1,))
            add_squares(6, (3,))
        if last_stage >= 7:
            ffn(2, 6, "n6", lambda k: gmod[:, 8 + k:9 + k], 24)

        res = token_view(ybuf)
        for q in range(4):
            a, h = q % 2, q // 2
            dve.wait_ge(out_turned, q + 1)
            dve.tensor_copy(res[:, a, h * 512:(h + 1) * 512], ps[:, 4 + q, :]).then_inc(out_made, 1)

    @block.tensor
    def _(pe):
        def g_step(g, hi, lo, ready, tokens_out=False, slots=None, bank=None, waited=False):
            slot = g % 2
            b = gbank(g)
            if not waited:
                pe.wait_ge(g_hi_made, g + 1)
                pe.wait_ge(g_lo_made, g + 1)
                if g >= 4:
                    g_free(g - 4)
            for k in range(KT):
                ready(k)
                for a in range(2):
                    for n, (w, x) in enumerate(((g_hi, hi), (g_hi, lo), (g_lo, hi))):
                        wt, xt = w[:, slot, k, :], x[:, k, :]
                        st = dict(start=(k == 0 and a == 0 and n == 0), stop=(k == KT - 1 and n == 2),
                                  skip_group_check=True)
                        if tokens_out:
                            mm = pe.matmul(pair(b)[:, a, :], xt[:, a * P:(a + 1) * P], wt, **st)
                        else:
                            mm = pe.matmul(pair(b)[:, a, :], wt[:, a * P:(a + 1) * P], xt, **st)
            mm.then_inc(g_done, 1)

        def g_free(g):
            for f, first in enumerate(FFNS):
                if first <= g < first + FT:
                    pe.wait_ge(hid_made, FT * f + g - first + 1)
                    return
            if MX_OG <= g < MX_OG + 2:
                pe.wait_ge(og_made, g - MX_OG + 1)
                return
            pe.wait_ge(g_evac, evacs(g))

        def no_wait(k):
            pass

        def filled(signal, before, per=1):
            return lambda k: pe.wait_ge(signal, before + k // per + 1)

        def a_filled(fill):
            return filled(opa_made, 8 * A_FILL[fill])

        def sum_squares(n):
            pe.wait_ge(sq_added, n + 1)
            src, at = (qk_m, T) if n == 5 else (ybuf, 0)
            for k in range(2):
                mm = pe.matmul(ps[:, 0, at:at + T], ones[:, :], src[:, k, :], start=(k == 0), stop=(k == 1))
            mm.then_inc(ss_done, 1)

        def ffn(f, norm, hi, lo, ready):
            g0, d0 = FFNS[f], FT * f
            if f < 2:
                g_step(g0, hi, lo, ready)
            sum_squares(norm)
            if f == 1:
                pe.wait_ge(ada_added, 6 * KT)
                for c in range(48):
                    mm = pe.matmul(ps[:, 1, c:c + 1], ada_acc[:, c * P:(c + 1) * P], ones[:, 0:1], start=True, stop=True)
                mm.then_inc(ada_summed, 1)
            if f == 2:
                g_step(g0, hi, lo, ready)

            def d_step(i, r, s):
                if f == 1 and s == 0:
                    pe.wait_ge(mod_made, 2)
                pe.wait_ge(d_hi_made, i * 4 + (d0 + r + 1))
                pe.wait_ge(d_lo_made, i * 4 + (d0 + r + 1))
                pe.wait_ge(hid_lo_made, i * 4 + (d0 + r + 1))
                for a in range(KT):
                    for n, (w, x) in enumerate(((d_hi, hid_hi), (d_hi, hid_lo), (d_lo, hid_hi))):
                        mm = pe.matmul(pair(a // 2)[:, a % 2, :], w[:, r % 2, a * P:(a + 1) * P], x[:, r % 2, :],
                                       start=(s == 0 and a % 2 == 0 and n == 0), stop=(s == FT - 1 and n == 2),
                                       skip_group_check=True)
                mm.then_inc(d_done, 1)

            def both(i, r, s):
                pe.wait_ge(g_hi_made, i * 4 + (g0 + r + 2))
                pe.wait_ge(g_lo_made, i * 4 + (g0 + r + 2))
                if s is None or s >= 3:
                    pe.wait_ge(hid_made, i * 4 + (d0 + r - 2))
                else:
                    g_free(g0 + s + 1 - 4)
                g_step(g0 + r + 1, hi, lo, no_wait, waited=True)
                d_step(i, r, s)

            for r in range(4):
                both(0, r, r)
            with pe.Fori(1, 5) as i:
                for r in range(4):
                    both(i, r, None)
            both(5, 0, 20)
            d_step(5, 1, 21)

        pe.wait_ge(consts, c_basic)
        pe.wait_ge(x_loaded, 16)
        x_tok = token_view(ybuf)
        for k in range(KT):
            for a in range(TT):
                mm = pe.transpose(pair(k // 2)[:, k % 2, a * P:(a + 1) * P], x_tok[:, a, k * P:(k + 1) * P], ident[:, :])
            if k % 2 == 1:
                mm.then_inc(x_turned, 1)
        pe.wait_ge(par_loaded, 16 * N_PARAM_DMAS)
        pe.transpose(ps[:, 4, 0:P], prow[:, 0, :], ident[:, :])
        pe.transpose(ps[:, 4, P:NROWS], prow[0:NROWS - P, 1, :], ident[0:NROWS - P, 0:NROWS - P]).then_inc(par_turned, 1)

        for s in range(8):
            g_step(CV + s, opa_hi, opa_lo, a_filled("n0") if s == 0 else no_wait)
            if s == 0:
                sum_squares(0)
        for s in range(4):
            g_step(BG + s, opa_hi, opa_lo, no_wait)
        for s in range(4):
            g_step(AO + s, opb_hi, opb_lo, filled(opb_made, 0, 2))
        if last_stage >= 2:
            ffn(0, 1, opa_hi, opa_lo, a_filled("n1"))

        if last_stage >= 3:
            for s in range(6):
                g_step(KV + s, opa_hi, opa_lo, a_filled("n2") if s == 0 else no_wait, tokens_out=s in (3, 5))
                if s == 0:
                    sum_squares(2)
                if s == 2:
                    pe.wait_ge(g_evac, evacs(KV))
                    for a in range(TT):
                        mm = pe.transpose(ps[:, 1, a * P:(a + 1) * P], rstd[:, a * P:(a + 1) * P], ident[:, :])
                    mm.then_inc(r_turned, 1)

            def cmp_hidden(w):
                c = CHUNKS.index(("cmp", w))
                pe.wait_ge(b_cmp_made, 2 * w + 2)
                pe.wait_ge(g_loaded[c % 2], 32 * (c // 2 + 1))
                for a in range(2):
                    for l in range(16):
                        mm = pe.matmul(ps[:, w, a * 64:(a + 1) * 64], w1_view(c % 2)[:, l, a * P:(a + 1) * P],
                                       b_cmp[:, l, :, :].rearrange("p g n -> p (g n)"), start=(l == 0), stop=(l == 15))
                mm.then_inc(cmp_hid_done, 1)

            for s in range(4):
                g_step(QG + s, opb_hi, opb_lo, filled(opb_made, B_FILL["b"]) if s == 0 else no_wait)
            cmp_hidden(0)
            pe.wait_ge(side_lo, 2)
            for k in range(KT):
                for n, (w, x) in enumerate(((qg_hi, opb_hi), (qg_hi, opb_lo), (qg_lo, opb_hi))):
                    mm = pe.matmul(ps[0:48, 3, 0:T], w[:, k, :], x[:, k, :],
                                   start=(k == 0 and n == 0), stop=(k == KT - 1 and n == 2))
            mm.then_inc(gate_done, 1)
            cmp_hidden(1)
            pe.wait_ge(gate_exp, 1)
            for a in range(TT):
                mm = pe.transpose(ps[:, 3, 256 + 48 * a:304 + 48 * a], gate_row[:, a * P:(a + 1) * P], ident[0:48, 0:48])
            mm.then_inc(gate_turned, 1)
            pe.wait_ge(cmp_hid_silu, 3)
            pe.wait_ge(w2_loaded, 48)
            for a in range(2):
                pe.matmul(ps[:, 2, 0:64], w2_k[:, a, :, :].rearrange("p w n -> p (w n)"),
                          hid_cmp[:, 0, a, :, :].rearrange("p g n -> p (g n)"), start=(a == 0), stop=(a == 1))
            for half in range(2):
                for a in range(2):
                    mm = pe.matmul(ps[:, 2, HD * (1 + half):HD * (2 + half)], vrep[:, a, half * P:(half + 1) * P],
                                   w2_v[:, a, :], start=(a == 0), stop=(a == 1))
            mm.then_inc(kc_done, 1)
            pe.wait_ge(kc_made, 2)
            pe.wait_ge(g_evac, evacs(QG + 3))
            for j in range(NH // 2):
                for a in range(TT):
                    at = (a * NH + 2 * j) * 16
                    mm = pe.matmul(ps[:, 4, at:at + 32], q_t[:, j, a * P:(a + 1) * P],
                                   kc_blk[:, j // 2, :, :].rearrange("p b n -> p (b n)"), start=True, stop=True)
            mm.then_inc(cs_done, 1)
            def scores(h):
                if h >= 2:
                    pe.wait_ge(shifted, h - 1)
                lo, g = HD * (h % 2), h // 4
                for a, w in ((1, 256), (0, 128)):
                    for b in range(2):
                        mm = pe.matmul(ps[:, 2 * (h % 2) + (1 - a), b * w:(b + 1) * w],
                                       q_t[lo:lo + HD, h // 2, a * P:(a + 1) * P], k_dup[lo:lo + HD, b, g, 0:w],
                                       start=True, stop=True)
                mm.then_inc(scored, 1)

            pe.wait_ge(kc_made, 4)
            pe.wait_ge(gates_made, 1)
            scores(0)
            scores(1)
            pe.wait_ge(cs_made, 1)
            for q in range(2):
                for a in range(TT):
                    mm = pe.transpose(ps[:, 7, (2 * q + a) * P:(2 * q + a + 1) * P],
                                      ctmp[:, a * T + q * P:a * T + (q + 1) * P], ident[:, :])
            mm.then_inc(pct_done, 1)

            scores(2)
            for h in range(NH):
                pe.wait_ge(scaled, h + 1)
                if h >= 1:
                    pe.wait_ge(pt_slc, h)
                    pe.wait_ge(pt_win, h)
                e = e_buf[:, h % 3, :]
                for b in range(2):
                    for lo, at in ((512 + b * P, 0), (b * 256, P), (b * 256 + P, 2 * P)):
                        mm = pe.transpose(ps[:, 4 + b, at:at + P], e[:, lo:lo + P], ident[:, :])
                mm.then_inc(pt_done, 1)
                if h + 3 < NH:
                    scores(h + 3)
                pe.wait_ge(pt_slc, h + 1)
                pe.wait_ge(pt_win, h + 1)
                pe.wait_ge(pct_made, 1)
                j, lo, v = h // 2, HD * (h % 2), HD * (h // 4)
                if j >= 2:
                    pe.wait_ge(opa_made, 8 * A_FILL["attn"] + j - 1)
                o = ps[lo:lo + HD, 6 + j % 2, 0:T]
                n = 0
                for b in range(2):
                    for s, ob, pb in ((0, o, pt_buf[:, b, 0:256]), (1, o[:, P:T], pt_buf[:, b, 256:384])):
                        pe.matmul(ob, v_tok[:, b, s, v:v + HD], pb, start=(n == 0), stop=False, skip_group_check=True)
                        n += 1
                pe.matmul(o, vc_blk[:, h, :], pct[:, h // 8, :], start=False, stop=True,
                          skip_group_check=True).then_inc(pv_done, 1)
            for s in range(4):
                g_step(WO + s, opa_hi, opa_lo, a_filled("attn") if s == 0 else no_wait)
        if last_stage >= 4:
            ffn(1, 3, opb_hi, opb_lo, filled(opb_made, B_FILL["n3"]))

        if last_stage >= 5:
            sum_squares(4)
            sum_squares(5)
            pe.wait_ge(consts, c_comb)
            for a, lo, w in ((1, 0, 256), (0, 256, 128)):
                for i, r in ((0, 4), (1, 16)):
                    mm = pe.matmul(ps[:, 1, lo:lo + w], comb[0:r, i, a * P:(a + 1) * P], comb[0:r, i, 0:w],
                                   start=(i == 0), stop=(i == 1))
            mm.then_inc(comb_done, 1)
            for s in range(14):
                g = MX + s
                g_step(g, opa_hi, opa_lo, a_filled("n5") if s == 0 else no_wait,
                       tokens_out=MX_VA <= g < MX_QM or MX_VM <= g < MX_OG)
                if s == 0:
                    for i in range(2):
                        for k in range(KT):
                            for n, (w, x) in enumerate(((if_hi, opa_hi), (if_hi, opa_lo), (if_lo, opa_hi))):
                                mm = pe.matmul(ps[0:NM, 2, i * T:(i + 1) * T], w[:, k, NM * i:NM * i + NM], x[:, k, :],
                                               start=(k == 0 and n == 0), stop=(k == KT - 1 and n == 2))
                    mm.then_inc(if_done, 1)
                if 1 <= s < 5:
                    j = s - 1
                    pe.wait_ge(qk_sq, j + 1)
                    if j >= 2:
                        pe.wait_ge(qk_root, j - 1)
                    for k in (2 * j, 2 * j + 1):
                        mm = pe.matmul(pair(j % 2)[:, k % 2, :], ones64[:, :], ybuf[:, k, :], start=True, stop=True)
                    mm.then_inc(qk_ss, 1)
                if s == 8:
                    pe.wait_ge(rows_made, 1)
                    for a in range(TT):
                        mm = pe.transpose(ps[:, 2, NM * a:NM * a + NM], rows[:, 3, a * P:(a + 1) * P], ident[0:NM, 0:NM])
                    mm.then_inc(a_turned, 1)

        if last_stage >= 6:
            pe.wait_ge(qk_made, 4)

            def dil_scores(h):
                if h >= 2:
                    pe.wait_ge(shifted, NH + h - 1)
                lo, j = HD * (h % 2), h // 2
                for a, at, w in ((1, 0, 256), (0, 256, 128)):
                    mm = pe.matmul(ps[:, h % 2, at:at + w], qk_a[lo:lo + HD, j, a * P:(a + 1) * P],
                                   qk_a[lo:lo + HD, 4 + j, 0:w], start=True, stop=True)
                mm.then_inc(scored, 1)

            for h in range(3):
                dil_scores(h)
            for h in range(NH2):
                pe.wait_ge(scaled, NH + h + 1)
                if h >= 2:
                    pe.wait_ge(pt_slc, NH + h - 1)
                e = e_dil[:, h % 3, :]
                for lo, at in ((256, 0), (0, P), (P, 2 * P)):
                    mm = pe.transpose(ps[:, 4 + h % 2, at:at + P], e[:, lo:lo + P], ident[:, :])
                mm.then_inc(pt_done, 1)
                if h + 3 < NH2:
                    dil_scores(h + 3)
                pe.wait_ge(pt_slc, NH + h + 1)
                j, lo = h // 2, HD * (h % 2)
                if j >= 2:
                    pe.wait_ge(opa_made, 8 * A_FILL["mix"] + j - 1)
                o = ps[lo:lo + HD, 6 + j % 2, 0:T]
                pe.matmul(o, v_a[:, 0, h * HD:(h + 1) * HD], pt_dil[:, h % 2, 0:256], start=True, stop=False,
                          skip_group_check=True)
                pe.matmul(o[:, P:T], v_a[:, 1, h * HD:(h + 1) * HD], pt_dil[:, h % 2, 256:384], start=False, stop=True,
                          skip_group_check=True).then_inc(pv_done, 1)
            pe.wait_ge(shifted, NH + NH2)
            pe.wait_ge(pt_slc, NH + NH2)
            pe.wait_ge(conv_ready_made, 4)
            pe.wait_ge(opa_made, 8 * A_FILL["mix"] + 4)

            def lstm_squares(m):
                pe.wait_ge(lsq_made, m + 1)
                pe.matmul(ps[:, m, 0:T], ones[:, :], l_sq[:, m, :], start=True, stop=True).then_inc(lss_done, 1)

            pe.wait_ge(a_made, 1)
            for m in range(NM):
                for i in range(2):
                    mm = pe.matmul(ps[:, m, i * T:(i + 1) * T], sel4[:, m, :], rows[:, 5 + i, :], start=True, stop=True)
                mm.then_inc(m_cast, 1)
                q, k = qk_m[:, m, :], qk_m[:, 4 + m, :]
                pe.matmul(ps[:, 4 + m, 0:256], k[:, 0:P], q, start=True, stop=True)
                pe.matmul(ps[:, 4 + m, 256:384], k[:, P:T], q[:, P:T], start=True, stop=True).then_inc(ls_done, 1)
            for m in range(NM):
                pe.wait_ge(ls_made, m + 1)
                pe.wait_ge(emt_made, m + 1)
                for i in range(2):
                    for s in range(2):
                        w = v_m[:, s, m * P:(m + 1) * P] if i == 0 else ones[:, :]
                        o = ps[:, m, i * T + s * P:(i + 1) * T]
                        x = decay[:, m, 256 * s:256 + 128 * s]
                        mm = pe.matmul(o, w, x, start=(s == 0), stop=(s == 1), skip_group_check=True)
                mm.then_inc(num_done, 1)
                if m >= 1:
                    lstm_squares(m - 1)
            lstm_squares(NM - 1)
            for s in range(4):
                g_step(MO + s, opa_hi, opa_lo, a_filled("mix") if s == 0 else no_wait, waited=False)
        if last_stage >= 7:
            ffn(2, 6, opa_hi, opa_lo, a_filled("n6"))

        for q in range(4):
            pe_ready = {1: 1, 2: 2, 3: 3, 4: 4, 5: 5, 6: 6, 7: 7}[last_stage]
            piece_ready(pe, pe_ready, 2 * (q // 2) + 1)
            a = q % 2
            for k in range(4 * (q // 2), 4 * (q // 2) + 4):
                mm = pe.transpose(ps[:, 4 + q, (k % 4) * P:(k % 4 + 1) * P], xres[:, k, a * P:(a + 1) * P], ident[:, :])
            mm.then_inc(out_turned, 1)
    return ctx


_OUT = (1, T, D)


def kernel(**inputs):
    import numpy as np
    import concourse.bacc as bacc
    from concourse.bass_utils import run_bass_kernel_spmd

    nc = bacc.Bacc("TRN2", target_bir_lowering=False, num_devices=1)
    arrays, t = {}, {}
    for name, value in inputs.items():
        a = np.ascontiguousarray(value)
        arrays["in_" + name] = a
        t[name] = nc.dram_tensor("in_" + name, a.shape, mybir.dt.from_np(a.dtype), kind="ExternalInput").ap()
    out = nc.dram_tensor("out_x", _OUT, F32, kind="ExternalOutput").ap()
    with layer_kernel(nc, t, out):
        pass
    r = run_bass_kernel_spmd(nc, [arrays], core_ids=[0])
    return r.results[0]["out_x"]
```
